# Optimizing a Trainium2 kernel written in Bass

```python
import jax, jax.numpy as jnp
from jax import lax
import numpy as np

D_MODEL = 1024
BATCH = 1
SEQ = 256
DEPTH = 2

GRID_W = 64
NA_HEADS = 16
NA_HEAD_DIM = D_MODEL // NA_HEADS
WIN_H = 8
WIN_W = 16
GQA_Q_HEADS = 16
GQA_KV_HEADS = 4
GQA_HEAD_DIM = D_MODEL // GQA_Q_HEADS
ROPE_THETA = 10000.0
Q_BLOCK = 128
D_FF = D_MODEL * 7 // 2
N_EXPERTS = 8
TOP_K = 2
EPS = 1e-6
N_EVEN = (DEPTH + 1) // 2
N_ODD = DEPTH // 2

kernel_name = "hybrid_natten_axial_gqa_moe_encoder"

def rmsnorm(x, g):
    xf = x.astype(jnp.float32)
    y = xf * lax.rsqrt(jnp.mean(xf * xf, axis=-1, keepdims=True) + EPS)
    return (y * g.astype(jnp.float32)).astype(x.dtype)

def rope_1d(x, pos):
    half = x.shape[-1] // 2
    freqs = ROPE_THETA ** (-jnp.arange(half, dtype=jnp.float32) / half)
    ang = pos.astype(jnp.float32)[:, None] * freqs[None, :]
    cos = jnp.cos(ang)[:, None, :]
    sin = jnp.sin(ang)[:, None, :]
    xf = x.astype(jnp.float32)
    x1, x2 = xf[..., :half], xf[..., half:]
    out = jnp.concatenate([x1 * cos - x2 * sin, x2 * cos + x1 * sin], axis=-1)
    return out.astype(x.dtype)

def axial_rope(x, row_pos, col_pos):
    half = x.shape[-1] // 2
    return jnp.concatenate([rope_1d(x[..., :half], row_pos),
                            rope_1d(x[..., half:], col_pos)], axis=-1)

def swiglu(h, w_gate, w_up, w_down):
    return (jax.nn.silu(h @ w_gate) * (h @ w_up)) @ w_down

def neighborhood_attention(h, w_qkv, rpb, w_o):
    B, S, D = h.shape
    rows = S // GRID_W
    kh = min(WIN_H, rows)
    qkv = (h @ w_qkv).reshape(B, rows, GRID_W, 3, NA_HEADS, NA_HEAD_DIM)
    q = qkv[..., 0, :, :] * (NA_HEAD_DIM ** -0.5)
    k = qkv[..., 1, :, :]
    v = qkv[..., 2, :, :]
    cols = jnp.arange(GRID_W)
    col_start = jnp.clip(cols - WIN_W // 2, 0, GRID_W - WIN_W)
    col_idx = col_start[:, None] + jnp.arange(WIN_W)[None, :]
    col_off = col_idx - cols[:, None] + (WIN_W - 1)

    def row_step(args):
        q_r, r = args
        rs = jnp.clip(r - kh // 2, 0, rows - kh)
        k_band = lax.dynamic_slice_in_dim(k, rs, kh, axis=1)
        v_band = lax.dynamic_slice_in_dim(v, rs, kh, axis=1)
        k_nb = k_band[:, :, col_idx]
        v_nb = v_band[:, :, col_idx]
        row_off = rs + jnp.arange(kh) - r + (WIN_H - 1)
        bias = rpb[:, row_off[None, :, None], col_off[:, None, :]]
        s = jnp.einsum('bqhd,biqjhd->bhqij', q_r, k_nb).astype(jnp.float32)
        s = s + bias.astype(jnp.float32)[None]
        p = jax.nn.softmax(s.reshape(B, NA_HEADS, GRID_W, kh * WIN_W), axis=-1)
        p = p.reshape(B, NA_HEADS, GRID_W, kh, WIN_W).astype(v.dtype)
        return jnp.einsum('bhqij,biqjhd->bqhd', p, v_nb)

    o = lax.map(row_step, (q.transpose(1, 0, 2, 3, 4), jnp.arange(rows)))
    o = o.transpose(1, 0, 2, 3, 4).reshape(B, S, NA_HEADS * NA_HEAD_DIM)
    return o @ w_o

def axial_gqa(h, w_qkv, q_g, k_g, w_o):
    B, S, D = h.shape
    nq = GQA_Q_HEADS * GQA_HEAD_DIM
    nkv = GQA_KV_HEADS * GQA_HEAD_DIM
    groups = GQA_Q_HEADS // GQA_KV_HEADS
    qkv = h @ w_qkv
    q = qkv[..., :nq].reshape(B, S, GQA_Q_HEADS, GQA_HEAD_DIM)
    k = qkv[..., nq:nq + nkv].reshape(B, S, GQA_KV_HEADS, GQA_HEAD_DIM)
    v = qkv[..., nq + nkv:].reshape(B, S, GQA_KV_HEADS, GQA_HEAD_DIM)
    q = rmsnorm(q, q_g)
    k = rmsnorm(k, k_g)
    t = jnp.arange(S)
    row_pos = t // GRID_W
    col_pos = t % GRID_W
    q = axial_rope(q, row_pos, col_pos) * (GQA_HEAD_DIM ** -0.5)
    k = axial_rope(k, row_pos, col_pos)
    nb = S // Q_BLOCK
    qb = q.reshape(B, nb, Q_BLOCK, GQA_KV_HEADS, groups, GQA_HEAD_DIM).transpose(1, 0, 2, 3, 4, 5)

    def block(q_blk):
        s = jnp.einsum('bqkgd,bskd->bkgqs', q_blk, k).astype(jnp.float32)
        p = jax.nn.softmax(s, axis=-1).astype(v.dtype)
        return jnp.einsum('bkgqs,bskd->bqkgd', p, v)

    o = lax.map(block, qb)
    o = o.transpose(1, 0, 2, 3, 4, 5).reshape(B, S, nq)
    return o @ w_o

def moe_swiglu(h, w_router, w_gate, w_up, w_down):
    B, S, D = h.shape
    ht = h.reshape(B * S, D)
    logits = (ht @ w_router).astype(jnp.float32)
    top_vals, top_idx = lax.top_k(logits, TOP_K)
    gates = jax.nn.softmax(top_vals, axis=-1)
    gate_full = jnp.sum(jax.nn.one_hot(top_idx, N_EXPERTS, dtype=jnp.float32) * gates[..., None], axis=1)
    y = jnp.zeros((B * S, D), jnp.float32)
    for e in range(N_EXPERTS):
        y = y + gate_full[:, e:e + 1] * swiglu(ht, w_gate[e], w_up[e], w_down[e]).astype(jnp.float32)
    return y.astype(h.dtype).reshape(B, S, D)

def setup_inputs(seed: int = 0) -> dict:
    key = jax.random.key(seed)
    ks = jax.random.split(key, 16)
    f32 = jnp.float32
    D = D_MODEL
    nq = GQA_Q_HEADS * GQA_HEAD_DIM
    nkv = GQA_KV_HEADS * GQA_HEAD_DIM
    def w(k, shape, fan_in):
        return jax.random.normal(k, shape, f32) * (fan_in ** -0.5)
    return {
        "x": jax.random.normal(ks[0], (BATCH, SEQ, D), f32),
        "norm_g": 1.0 + 0.05 * jax.random.normal(ks[1], (DEPTH, 4, D), f32),
        "na_w_qkv": w(ks[2], (N_EVEN, D, 3 * NA_HEADS * NA_HEAD_DIM), D),
        "na_rpb": 0.02 * jax.random.normal(ks[3], (N_EVEN, NA_HEADS, 2 * WIN_H - 1, 2 * WIN_W - 1), f32),
        "na_w_o": w(ks[4], (N_EVEN, NA_HEADS * NA_HEAD_DIM, D), NA_HEADS * NA_HEAD_DIM),
        "gqa_w_qkv": w(ks[5], (N_ODD, D, nq + 2 * nkv), D),
        "gqa_q_norm": 1.0 + 0.05 * jax.random.normal(ks[6], (N_ODD, GQA_HEAD_DIM), f32),
        "gqa_k_norm": 1.0 + 0.05 * jax.random.normal(ks[7], (N_ODD, GQA_HEAD_DIM), f32),
        "gqa_w_o": w(ks[8], (N_ODD, nq, D), nq),
        "ffn_w_gate": w(ks[9], (N_EVEN, D, D_FF), D),
        "ffn_w_up": w(ks[10], (N_EVEN, D, D_FF), D),
        "ffn_w_down": w(ks[11], (N_EVEN, D_FF, D), D_FF),
        "moe_w_router": w(ks[12], (N_ODD, D, N_EXPERTS), D),
        "moe_w_gate": w(ks[13], (N_ODD, N_EXPERTS, D, D_FF), D),
        "moe_w_up": w(ks[14], (N_ODD, N_EXPERTS, D, D_FF), D),
        "moe_w_down": w(ks[15], (N_ODD, N_EXPERTS, D_FF, D), D_FF),
    }

def reference(x, norm_g, na_w_qkv, na_rpb, na_w_o, gqa_w_qkv, gqa_q_norm, gqa_k_norm, gqa_w_o,
              ffn_w_gate, ffn_w_up, ffn_w_down, moe_w_router, moe_w_gate, moe_w_up, moe_w_down):
    h = x
    for i in range(DEPTH):
        j = i // 2
        a = rmsnorm(h, norm_g[i, 0])
        if i % 2 == 0:
            a = neighborhood_attention(a, na_w_qkv[j], na_rpb[j], na_w_o[j])
        else:
            a = axial_gqa(a, gqa_w_qkv[j], gqa_q_norm[j], gqa_k_norm[j], gqa_w_o[j])
        h = h + rmsnorm(a, norm_g[i, 1])
        f = rmsnorm(h, norm_g[i, 2])
        if i % 2 == 0:
            f = swiglu(f, ffn_w_gate[j], ffn_w_up[j], ffn_w_down[j])
        else:
            f = moe_swiglu(f, moe_w_router[j], moe_w_gate[j], moe_w_up[j], moe_w_down[j])
        h = h + rmsnorm(f, norm_g[i, 3])
    return h


_drawn_inputs = setup_inputs


def setup_inputs(seed=0):
    import zlib

    import numpy as np

    out = dict(_drawn_inputs(seed))
    spreads = {}
    factors = {}
    for name, (base, spread) in spreads.items():
        noise = np.random.default_rng([zlib.crc32(name.encode()), seed]).standard_normal(out[name].shape)
        drawn = base * np.exp(spread * noise) if base else spread * noise
        out[name] = __import__('jax').numpy.asarray(drawn.astype(out[name].dtype))
    for name, factor in factors.items():
        out[name] = (out[name] * factor).astype(out[name].dtype)
    return out
```

```python
from contextlib import ExitStack

import numpy as np

import concourse.bass as bass
from concourse import mybir

F32 = mybir.dt.float32
F32R = mybir.dt.float32r
I32 = mybir.dt.int32
ACT = mybir.ActivationFunctionType
ALU = mybir.AluOpType
AX = mybir.AxisListType

P = 128
D = 1024
SEQ = 256
T = SEQ // P
KC = D // P
GRID_W = 64
ROWS = SEQ // GRID_W
HEADS = 16
HD = 64
KV_HEADS = 4
WIN_H, WIN_W = 8, 16
RPB_H, RPB_W = 2 * WIN_H - 1, 2 * WIN_W - 1
D_FF = D * 7 // 2
E = 8
TOP_K = 2
EPS = 1e-6
NQ = HEADS * HD
NKV = KV_HEADS * HD
QKV1 = NQ + 2 * NKV
NORM_HEADS = HEADS + KV_HEADS
MASKED = -1e30

COLS = 512
PK = 4
RAW = 6
SPLIT = 3
STEPS = D_FF // COLS
FFN_PIECES = 6 * STEPS

Q0 = 0
O0 = Q0 + 2 * (3 * D // COLS)
F0 = O0 + 2 * (D // COLS)
Q1 = F0 + FFN_PIECES
O1 = Q1 + 2 * (QKV1 // COLS)
J0 = O1 + 2 * (D // COLS)

MAX_OVER = TOP_K * SEQ // (P + 1)
JOB_COLS = E + MAX_OVER + 1

C_IDENT, C_IOTA, C_BEFORE, C_ONES = 0, P, 2 * P, 3 * P
C_TRI = 4 * P
C_EXP = C_TRI + E * E
C_COS = C_EXP + E
C_SIN = C_COS + T * HD
C_ALL = C_SIN + T * HD


def constants():
    c = np.zeros((P, C_ALL), np.float32)
    c[:, C_IDENT:C_IDENT + P] = np.eye(P)
    c[:, C_IOTA:C_IOTA + P] = np.arange(P)
    c[:, C_BEFORE:C_BEFORE + P] = np.triu(np.ones((P, P)), 1)
    c[:, C_ONES:C_ONES + P] = 1.0
    c[:, C_TRI:C_TRI + E * E] = np.tril(np.ones((E, E)), -1).reshape(1, -1)
    c[:, C_EXP:C_EXP + E] = np.arange(E)
    quarter = HD // 4
    freqs = (np.float32(10000.0) ** (-np.arange(quarter, dtype=np.float32) / np.float32(quarter))).astype(np.float32)
    for t in range(T):
        tok = t * P + np.arange(P)
        for axis, pos in enumerate((tok // GRID_W, tok % GRID_W)):
            ang = pos.astype(np.float32)[:, None] * freqs[None, :]
            a = axis * HD // 2
            cos, sin = C_COS + t * HD + a, C_SIN + t * HD + a
            c[:, cos:cos + quarter] = c[:, cos + quarter:cos + 2 * quarter] = np.cos(ang)
            c[:, sin:sin + quarter] = -np.sin(ang)
            c[:, sin + quarter:sin + 2 * quarter] = np.sin(ang)
    return c


def first_piece(s):
    return 0 if s == 0 else 4 + 6 * (s - 1)


def encoder_kernel(nc, x, norm_g, na_w_qkv, na_rpb, na_w_o, gqa_w_qkv, gqa_q_norm, gqa_k_norm, gqa_w_o,
                   ffn_w_gate, ffn_w_up, ffn_w_down, moe_w_router, moe_w_gate, moe_w_up, moe_w_down,
                   consts, out):
    ctx = ExitStack()
    with ctx:
        def sb(name, shape, dt=F32, scope=None):
            return (scope or ctx).enter_context(nc.sbuf_tensor(name, shape, dt))

        def sem(name):
            return ctx.enter_context(nc.semaphore(name))

        raw = sb("raw", [P, RAW, PK, COLS])
        w_hi = sb("w_hi", [P, SPLIT, PK, COLS], F32R)
        w_lo = sb("w_lo", [P, SPLIT, PK, COLS], F32R)
        h = sb("h", [P, T, D])
        nrm = sb("nrm", [P, T, D])
        act_hi = sb("act_hi", [P, KC, SEQ], F32R)
        act_lo = sb("act_lo", [P, KC, SEQ], F32R)
        gain = sb("gain", [P, 2, D])
        cst = sb("cst", [P, C_ALL])
        small = sb("small", [P, 64])
        ident = cst[:, C_IDENT:C_IDENT + P]
        sumsq, meansq, std, rstd = (small[:, 4 * i:4 * i + 2] for i in range(4))
        nmax = small[:, 16:24].rearrange("p (b s) -> p b s", b=2)
        psums = small[:, 24:32].rearrange("p (b s) -> p b s", b=2)
        rsums = small[:, 32:40].rearrange("p (b s) -> p b s", b=2)
        attn = ExitStack()
        qT = sb("qT", [P, KC, SEQ], F32, attn)
        kT = sb("kT", [P, KC, SEQ], F32, attn)
        sc = sb("sc", [P, 2, 4, SEQ], F32, attn)
        pT = sb("pT", [P, 2, 8, P], F32, attn)
        layer0 = ExitStack()
        v0 = sb("v0", [P, T, D], F32, layer0)
        bias = sb("bias", [P, HEADS, ROWS + 2, GRID_W], F32, layer0)
        layer0.close()
        layer1 = ExitStack()
        qkv = sb("qkv", [P, T, QKV1], F32, layer1)
        rot_a = sb("rot_a", [P, NORM_HEADS * HD], F32, layer1)
        rot_b = sb("rot_b", [P, NORM_HEADS * HD], F32, layer1)
        kdup = sb("kdup", [P, KV_HEADS, 2, HD], F32, layer1)
        qk_gain = sb("qk_gain", [P, 2, HD], F32, layer1)
        qk_cos = sb("qk_cos", [P, 2, HD], F32, layer1)
        qk_sin = sb("qk_sin", [P, 2, HD], F32, layer1)
        head_ms = sb("head_ms", [P, NORM_HEADS], F32, layer1)
        head_std = sb("head_std", [P, NORM_HEADS], F32, layer1)
        head_rs = sb("head_rs", [P, NORM_HEADS], F32, layer1)
        layer1.close()
        attn.close()
        ffn = ExitStack()
        hid = sb("hid", [P, T, COLS], F32, ffn)
        sil = sb("sil", [P, T, COLS], F32, ffn)
        hT_hi = sb("hT_hi", [P, 2, T, PK * P], F32R, ffn)
        hT_lo = sb("hT_lo", [P, 2, T, PK * P], F32R, ffn)
        tok_hi = sb("tok_hi", [P, T, D], F32R, ffn)
        tok_lo = sb("tok_lo", [P, T, D], F32R, ffn)
        y_sb = sb("y_sb", [P, D], F32, ffn)
        fT = sb("fT", [P, KC, SEQ], F32, ffn)
        pick = sb("pick", [P, T, P], F32R, ffn)
        pick_g = sb("pick_g", [P, T, P], F32, ffn)
        pick_gT = sb("pick_gT", [P, T, P], F32, ffn)
        wr = sb("wr", [P, KC, E], F32, ffn)
        logit = sb("logit", [P, T, E], F32, ffn)
        pair = sb("pair", [P, T, E, E], F32, ffn)
        pair2 = sb("pair2", [P, T, E, E], F32, ffn)
        chosen = sb("chosen", [P, T, E], F32, ffn)
        gate = sb("gate", [P, T, E], F32, ffn)
        pos = sb("pos", [P, T, E], F32, ffn)
        r8 = sb("r8", [P, 6, E], F32, ffn)
        r1 = sb("r1", [P, 16], F32, ffn)
        prod8 = sb("prod8", [P, T, E], F32, ffn)
        job_pos = sb("job_pos", [P, T, JOB_COLS], F32, ffn)
        job_gate = sb("job_gate", [P, T, JOB_COLS], F32, ffn)
        cur = sb("cur", [P, 2, T], F32, ffn)
        over_f = sb("over_f", [P, 1 + MAX_OVER], F32, ffn)
        over = sb("over", [P, 1 + MAX_OVER], I32, ffn)
        ffn.close()
        ps = ctx.enter_context(nc.psum_tensor("ps", [P, 8, COLS], F32))

        landed = [sem(f"piece_landed_{i}") for i in range(RAW)]
        hi_ready, lo_ready, piece_used = sem("hi_ready"), sem("lo_ready"), sem("piece_used")
        x_in, cst_in, gain_in = sem("x_in"), sem("cst_in"), [sem("gain_in_0"), sem("gain_in_1")]
        bias_in, bias_masked, qk_gain_in, wr_in = sem("bias_in"), sem("bias_masked"), sem("qk_gain_in"), sem("wr_in")
        gain_used = sem("gain_used")
        sumsq_ready, meansq_ready, std_ready = sem("sumsq_ready"), sem("meansq_ready"), sem("std_ready")
        nrm_ready, nrm_turned, act_hi_ready, act_ready = (
            sem("nrm_ready"), sem("nrm_turned"), sem("act_hi_ready"), sem("act_ready"))
        h_ready = sem("h_ready")
        dve_chain = sem("dve_chain")
        qkv_ready, qkv_kept = [sem("qkv0_ready"), sem("qkv1_ready")], [sem("qkv0_kept"), sem("qkv1_kept")]
        att = [{n: sem(f"{n}_{i}") for n in (
            "scores_ready", "biased", "max_ready", "exp_ready", "probs_ready", "probs_turned", "pT_ready",
            "o_ready", "o_hi_ready", "o_split")} for i in range(2)]
        proj_ready = sem("proj_ready")
        heads_ms, heads_std, heads_ready, heads_turned, heads_kept = (
            sem("heads_ms"), sem("heads_std"), sem("heads_ready"), sem("heads_turned"), sem("heads_kept"))
        f0 = {n: sem(f"ffn_{n}") for n in ("gu", "silu", "hid", "turned", "hT_hi", "hT", "y")}
        fj = {n: sem(f"job_{n}") for n in ("gu", "silu", "hid", "turned", "hT_hi", "hT", "y")}
        tok_hi_ready, tok_ready, fT_ready, logits_ready = (
            sem("tok_hi_ready"), sem("tok_ready"), sem("fT_ready"), sem("logits_ready"))
        logits_kept, logits_exp, chosen_ready, pos_ready, over_ready = (
            sem("logits_kept"), sem("logits_exp"), sem("chosen_ready"), sem("pos_ready"), sem("over_ready"))
        cur_ready, pick_ready, gathered, x_hi_ready, x_ready = (
            sem("cur_ready"), sem("pick_ready"), sem("gathered"), sem("x_hi_ready"), sem("x_ready"))
        pick_turned, pickT_ready, y_kept, scattered, y_added = (
            sem("pick_turned"), sem("pickT_ready"), sem("y_kept"), sem("scattered"), sem("y_added"))
        out_stored = sem("out_stored")

        def rows_of(ap):
            return ap.rearrange("p b (r c) -> p b r c", c=GRID_W)[:, :, :, ::-1]

        def outputs(layer, u, acts):
            a, t = u // 2, u % 2
            dst = acts[:, 2 * a:2 * a + 2, t * P:(t + 1) * P]
            src = ps[:, 6 + u % 2, 0:2 * P].rearrange("p (b n) -> p b n", b=2)
            if layer == 0:
                return dst.rearrange("p b (r c) -> p b r c", c=GRID_W), rows_of(src)
            return dst, src

        def w_piece(w, k0, c0):
            return w[k0:k0 + PK * P, c0:c0 + COLS].rearrange("(b p) n -> p b n", p=P)

        def columns_then_halves(w, width):
            return [(w, half * PK * P, c0) for c0 in range(0, width, COLS) for half in range(2)]

        def swiglu_pieces(w_gate, w_up, w_down):
            pieces = []
            for s in range(STEPS + 1):
                if s < STEPS:
                    for w in (w_gate, w_up):
                        pieces += [(w, half * PK * P, s * COLS) for half in range(2)]
                if s >= 1:
                    pieces += [(w_down, (s - 1) * COLS, half * COLS) for half in range(2)]
            return pieces

        front = (columns_then_halves(na_w_qkv[0], 3 * D) + columns_then_halves(na_w_o[0], D)
                 + swiglu_pieces(ffn_w_gate[0], ffn_w_up[0], ffn_w_down[0])
                 + columns_then_halves(gqa_w_qkv[0], QKV1) + columns_then_halves(gqa_w_o[0], D))
        assert len(front) == J0 and FFN_PIECES % RAW == 0 and FFN_PIECES % SPLIT == 0

        block = ctx.enter_context(nc.Block())

        @block.sync
        def _(sp):
            def load(n, src, job=0):
                if not isinstance(n, int) or n >= RAW or not isinstance(job, int):
                    sp.wait_ge(lo_ready, job * FFN_PIECES + n - RAW + 1)
                sp.dma_start(raw[:, n % RAW, :, :], src).then_inc(landed[n % RAW], 16)

            def load_expert(job, expert):
                pieces = swiglu_pieces(moe_w_gate[0, expert], moe_w_up[0, expert], moe_w_down[0, expert])
                for i, piece in enumerate(pieces):
                    load(J0 + i, w_piece(*piece), job)

            sp.dma_start(h[:], x[0].rearrange("(t p) d -> p t d", p=P)).then_inc(x_in, 16)
            for n, piece in enumerate(front):
                load(n, w_piece(*piece))
            with sp.Fori(0, E) as e:
                load_expert(e, e)
            sp.wait_ge(over_ready, 1)
            n_over = sp.value_load(over[0:1, 0:1], min_val=0, max_val=MAX_OVER)
            with sp.If(n_over > 0):
                with sp.Fori(0, n_over) as i:
                    e = sp.value_load(over[0:1, bass.ds(i + 1, 1)], min_val=0, max_val=E - 1)
                    load_expert(i + E, e)
            for t in range(T):
                sp.wait_ge(h_ready, 4 * T - T + t + 1)
                sp.dma_start(out[0, t * P:(t + 1) * P, :], h[:, t, :]).then_inc(out_stored, 16)
            sp.wait_ge(out_stored, 16 * T)

        @block.gpsimd
        def _(pool):
            def load_gain(k):
                if k >= 2:
                    pool.wait_ge(gain_used, k - 1)
                g = norm_g[k // 4, k % 4:k % 4 + 1, :]
                pool.dma_start(gain[:, k % 2, :], g.to_broadcast([P, D])).then_inc(gain_in[k % 2], 16)

            pool.dma_start(cst[:], consts).then_inc(cst_in, 16)
            load_gain(0)
            load_gain(1)
            for a in range(2):
                for i in range(ROWS + 2):
                    src = bass.AP(na_rpb.tensor, (WIN_H - ROWS + 1 - a + i) * RPB_W + WIN_W - GRID_W,
                                  [[1, GRID_W], [RPB_H * RPB_W, HEADS], [1, GRID_W]])
                    pool.dma_start(bias[a * GRID_W:(a + 1) * GRID_W, :, i, :], src).then_inc(bias_in, 16)
            pool.wait_ge(bias_in, 2 * (ROWS + 2) * 16)
            edge = GRID_W - WIN_W
            for a in range(2):
                b = bias[a * GRID_W:(a + 1) * GRID_W].rearrange("p h i k -> p (h i) k")
                rows = HEADS * (ROWS + 2)
                pool.affine_select(out=b[:, :, 0:edge], in_=b[:, :, 0:edge], compare_op=ALU.is_ge, fill=MASKED,
                                   base=WIN_W // 2 - GRID_W + 1, pattern=[[0, rows], [1, edge]],
                                   channel_multiplier=1
                                   ).then_inc(bias_masked, 1)
                pool.wait_ge(bias_masked, 2 * a + 1)
                pool.affine_select(out=b[:, :, WIN_W:], in_=b[:, :, WIN_W:], compare_op=ALU.is_ge, fill=MASKED,
                                   base=WIN_W // 2 - 1 - WIN_W + GRID_W - 1, pattern=[[0, rows], [-1, edge]],
                                   channel_multiplier=-1).then_inc(bias_masked, 1)
            for k in range(2, 5):
                load_gain(k)
            for i, g in enumerate((gqa_q_norm, gqa_k_norm)):
                pool.dma_start(qk_gain[:, i, :], g.to_broadcast([P, HD])).then_inc(qk_gain_in, 16)
            for k in range(5, 8):
                load_gain(k)
            pool.wait_ge(h_ready, 3 * T)
            pool.dma_start(wr[:], moe_w_router[0].rearrange("(b p) e -> p b e", p=P)).then_inc(wr_in, 16)

        @block.scalar
        def _(act):
            split_at = [0]

            def split_until(end, job=None):
                for n in range(split_at[0], end):
                    base = 0 if job is None else job
                    act.wait_ge(landed[n % RAW], (base * (FFN_PIECES // RAW) + n // RAW + 1) * 16)
                    if n >= SPLIT:
                        act.wait_ge(piece_used, base * FFN_PIECES + n - SPLIT + 1)
                    act.activation(w_hi[:, n % SPLIT], raw[:, n % RAW], ACT.Copy).then_inc(hi_ready, 1)
                split_at[0] = end

            def root(k, t):
                act.wait_ge(meansq_ready, T * k + t + 1)
                act.activation(std[:, t:t + 1], meansq[:, t:t + 1], ACT.Sqrt).then_inc(std_ready, 1)

            def sum_squares(k, t, src):
                act.activation(nrm[:, t, :], src, ACT.Square, accum_out=sumsq[:, t:t + 1]).then_inc(sumsq_ready, 1)

            def pre_norm(k, turned, bank):
                for t in range(T):
                    if k == 0 and t == 0:
                        act.wait_ge(x_in, 16)
                    if k > 0:
                        act.wait_ge(h_ready, T * (k // 2) - T + t + 1)
                    sum_squares(k, t, h[:, t, :])
                for t in range(T):
                    root(k, t)
                if k == 6:
                    return
                for b in range(2 * T):
                    t, c = b // 2, b % 2
                    act.wait_ge(nrm_turned, turned + b + 1)
                    act.activation(act_hi[:, 4 * c:4 * c + 4, t * P:(t + 1) * P],
                                   ps[:, bank + b, :].rearrange("p (c n) -> p c n", c=4), ACT.Copy
                                   ).then_inc(act_hi_ready, 1)

            def post_norm(k, bank):
                for t in range(T):
                    sum_squares(k, t, ps[:, bank + 2 * t:bank + 2 * t + 2, :].rearrange("p b n -> p (b n)"))
                for t in range(T):
                    root(k, t)

            def attention(i):
                s = att[i]
                units = 2 * HEADS // 4
                for u in range(units + 3):
                    if u >= 3:
                        act.wait_ge(s["o_ready"], u - 2)
                        dst, src = outputs(i, u - 3, act_hi)
                        act.activation(dst, src, ACT.Copy).then_inc(s["o_hi_ready"], 1)
                    if u < units:
                        act.wait_ge(s["max_ready"], u + 1)
                        if i == 1 and u >= 2:
                            act.wait_ge(s["probs_turned"], u - 1)
                        for q in range(4):
                            src = sc[:, u % 2, q, :] if i == 0 else ps[:, 2 * (u % 2) + q // 2,
                                                                      (q % 2) * SEQ:(q % 2 + 1) * SEQ]
                            last = act.activation(sc[:, u % 2, q, :], src, ACT.Exp, bias=nmax[:, u % 2, q:q + 1],
                                                  accum_out=psums[:, u % 2, q:q + 1])
                        last.then_inc(s["exp_ready"], 1)
                    if 1 <= u <= units:
                        act.wait_ge(s["probs_turned"], u)
                        if u >= 3:
                            act.wait_ge(s["o_ready"], u - 2)
                        act.activation(pT[:, (u - 1) % 2].rearrange("p a n -> p (a n)"),
                                       ps[:, 4:6, :].rearrange("p b n -> p (b n)"), ACT.Copy
                                       ).then_inc(s["pT_ready"], 1)

            act.wait_ge(cst_in, 16)
            pre_norm(0, 0, 0)
            for j in range(6):
                split_until(min(Q0 + 2 * j + 2 + 2, O0))
                act.wait_ge(qkv_ready[0], j + 1)
                b = 4 * (j % 2)
                if j < 4:
                    chunks = slice(4 * (j % 2), 4 * (j % 2) + 4)
                    if j < 2:
                        act.activation(qT[:, chunks, :].rearrange("p b (r c) -> p b r c", c=GRID_W),
                                       rows_of(ps[:, b:b + 4, 0:SEQ]), ACT.Copy, scale=HD ** -0.5
                                       ).then_inc(qkv_kept[0], 1)
                    else:
                        act.activation(kT[:, chunks, :], ps[:, b:b + 4, 0:SEQ], ACT.Copy).then_inc(qkv_kept[0], 1)
                else:
                    act.activation(v0[:, :, (j - 4) * COLS:(j - 3) * COLS], ps[:, b:b + 2, :], ACT.Copy
                                   ).then_inc(qkv_kept[0], 1)
            split_until(O0 + SPLIT)
            attention(0)
            split_until(F0)
            act.wait_ge(proj_ready, 1)
            post_norm(1, 0)
            split_until(F0 + SPLIT)
            pre_norm(2, 4, 4)
            for s in range(STEPS):
                last = first_piece(s) + 3
                split_until(F0 + last + 3)
                act.wait_ge(f0["gu"], s + 1)
                act.activation(sil[:], ps[:, 0:4:2, :], ACT.Silu).then_inc(f0["silu"], 1)
                if s > 0:
                    split_until(F0 + min(last + 4, FFN_PIECES))
                act.wait_ge(f0["turned"], s + 1)
                act.activation(hT_hi[:, s % 2], ps[:, 0:4:2, :], ACT.Copy).then_inc(f0["hT_hi"], 1)
            split_until(Q1)
            act.wait_ge(f0["y"], 1)
            post_norm(3, 4)
            split_until(Q1 + SPLIT)
            pre_norm(4, 8, 0)
            split_until(O1)
            act.wait_ge(qkv_ready[1], 1)
            for t in range(T):
                act.activation(qkv[:, t, :].rearrange("p (j n) -> p j n", j=3), ps[:, t:6:2, :], ACT.Copy
                               ).then_inc(qkv_kept[1], 1)
            for t in range(T):
                act.wait_ge(heads_ms, t + 1)
                act.activation(head_std[:], head_ms[:], ACT.Sqrt).then_inc(heads_std, 1)
                act.wait_ge(heads_turned, t + 1)
                act.activation(qT[:, :, t * P:(t + 1) * P],
                               ps[:, 0:2, :].rearrange("p b (c n) -> p (b c) n", c=4), ACT.Copy).then_inc(heads_kept, 1)
                act.activation(kT[:, 0:KV_HEADS, t * P:(t + 1) * P],
                               ps[:, 2, :].rearrange("p (c n) -> p c n", c=4), ACT.Copy).then_inc(heads_kept, 1)
            split_until(O1 + SPLIT)
            attention(1)
            split_until(J0)
            act.wait_ge(proj_ready, 2)
            post_norm(5, 0)
            split_until(J0 + SPLIT)
            pre_norm(6, 12, 4)
            for t in range(T):
                act.wait_ge(nrm_ready, T * 3 + t + 1)
                act.activation(tok_hi[:, t, :], nrm[:, t, :], ACT.Copy).then_inc(tok_hi_ready, 1)
            for b in range(2 * T):
                t, c = b // 2, b % 2
                act.wait_ge(nrm_turned, 12 + b + 1)
                act.activation(fT[:, 4 * c:4 * c + 4, t * P:(t + 1) * P],
                               ps[:, 4 + b, :].rearrange("p (c n) -> p c n", c=4), ACT.Copy).then_inc(fT_ready, 1)
            act.wait_ge(logits_kept, 1)
            for t in range(T):
                act.activation(gate[:, t, :], logit[:, t, :], ACT.Exp, bias=r1[:, t:t + 1]).then_inc(logits_exp, 1)

            def keep_gathered(j):
                act.wait_ge(gathered, j + 1)
                act.activation(act_hi[:, :, 0:P], ps[:, 6:8, :].rearrange("p b (c n) -> p (b c) n", c=4), ACT.Copy
                               ).then_inc(x_hi_ready, 1)

            def expert_job(j):
                split_at[0] = max(J0, J0 + SPLIT if isinstance(j, int) else J0)
                split_until(J0 + SPLIT, j)
                act.wait_ge(pick_turned, j + 1)
                if not isinstance(j, int):
                    act.wait_ge(scattered, j)
                act.activation(pick_gT[:], ps[:, 1, 0:T * P].rearrange("p (t n) -> p t n", t=T), ACT.Copy
                               ).then_inc(pickT_ready, 1)
                for s in range(STEPS):
                    split_until(J0 + 6 * s + (4 if s else 6), j)
                    act.wait_ge(fj["gu"], j * STEPS + s + 1)
                    act.activation(sil[:, 0, :], ps[:, 2 * (s % 2), :], ACT.Silu).then_inc(fj["silu"], 1)
                    split_until(J0 + min(6 * s + 8, FFN_PIECES), j)
                    act.wait_ge(fj["turned"], j * STEPS + s + 1)
                    act.activation(hT_hi[:, 0, 0, :], ps[:, 2 * (s % 2), :], ACT.Copy).then_inc(fj["hT_hi"], 1)
                keep_gathered(j + 1)
                act.wait_ge(fj["y"], j + 1)
                act.activation(y_sb[:], ps[:, 4:6, :].rearrange("p b n -> p (b n)"), ACT.Copy).then_inc(y_kept, 1)

            keep_gathered(0)
            expert_job(0)
            with act.Fori(1, E) as j:
                expert_job(j)
            act.wait_ge(over_ready, 1)
            n_over = act.value_load(over[0:1, 0:1], min_val=0, max_val=MAX_OVER)
            with act.If(n_over > 0):
                with act.Fori(0, n_over) as i:
                    expert_job(i + E)
            act.wait_ge(y_added, (n_over + (E + 1)) * T)
            for t in range(T):
                act.activation(fT[:, 4 * t:4 * t + 4, :].rearrange("p c n -> p (c n)"), nrm[:, t, :], ACT.Square,
                               accum_out=sumsq[:, t:t + 1]).then_inc(sumsq_ready, 1)
            for t in range(T):
                root(7, t)

        @block.vector
        def _(dve):
            split_at = [0]
            links = [0]

            def link(ins):
                links[0] += 1
                ins.then_inc(dve_chain, 1)
                dve.wait_ge(dve_chain, links[0])

            def split_until(end, job=None):
                for n in range(split_at[0], end):
                    base = 0 if job is None else job
                    dve.wait_ge(hi_ready, base * FFN_PIECES + n + 1)
                    dve.tensor_tensor(w_lo[:, n % SPLIT], raw[:, n % RAW], w_hi[:, n % SPLIT].bitcast(F32),
                                      ALU.subtract).then_inc(lo_ready, 1)
                split_at[0] = end

            def deviation(k, t):
                dve.wait_ge(sumsq_ready, T * k + t + 1)
                dve.tensor_scalar(meansq[:, t:t + 1], sumsq[:, t:t + 1], 1.0 / D, EPS, ALU.mult, ALU.add
                                  ).then_inc(meansq_ready, 1)

            def inverse(k, t):
                dve.wait_ge(std_ready, T * k + t + 1)
                link(dve.reciprocal(rstd[:, t:t + 1], std[:, t:t + 1]))

            def pre_norm(k, bank):
                dve.wait_ge(gain_in[0], 16 * (k // 2 + 1))
                for t in range(T):
                    deviation(k, t)
                for t in range(T):
                    inverse(k, t)
                    dve.scalar_tensor_tensor(nrm[:, t, :], h[:, t, :], rstd[:, t:t + 1], gain[:, 0, :],
                                             ALU.mult, ALU.mult).then_inc(nrm_ready, 1)
                dve.wait_ge(nrm_ready, T * (k // 2 + 1))
                dve.sem_inc(gain_used, 1)
                if k == 6:
                    return
                for b in range(2 * T):
                    t, c = b // 2, b % 2
                    dve.wait_ge(act_hi_ready, 2 * T * (k // 2) + b + 1)
                    dst = (slice(None), slice(4 * c, 4 * c + 4), slice(t * P, (t + 1) * P))
                    dve.tensor_tensor(act_lo[dst], ps[:, bank + b, :].rearrange("p (c n) -> p c n", c=4),
                                      act_hi[dst].bitcast(F32), ALU.subtract).then_inc(act_ready, 1)

            def post_norm(k, src):
                dve.wait_ge(gain_in[1], 16 * (k // 2 + 1))
                for t in range(T):
                    deviation(k, t)
                for t in range(T):
                    inverse(k, t)
                    link(dve.scalar_tensor_tensor(nrm[:, t, :], src(t), rstd[:, t:t + 1], gain[:, 1, :],
                                                  ALU.mult, ALU.mult))
                    dve.tensor_tensor(h[:, t, :], h[:, t, :], nrm[:, t, :], ALU.add).then_inc(h_ready, 1)
                dve.sem_inc(gain_used, 1)

            def from_banks(bank):
                return lambda t: ps[:, bank + 2 * t:bank + 2 * t + 2, :].rearrange("p b n -> p (b n)")

            def attention(i):
                s = att[i]
                units = 2 * HEADS // 4
                for u in range(units + 3):
                    if u < units:
                        a, t = u // 2, u % 2
                        dve.wait_ge(s["scores_ready"], u + 1)
                        banks = ps[:, 2 * (u % 2):2 * (u % 2) + 2, :]
                        if i == 0:
                            if u >= 2:
                                dve.wait_ge(s["probs_turned"], u - 1)
                            for par in range(2):
                                dve.tensor_tensor(
                                    sc[:, u % 2, 2 * par:2 * par + 2, :],
                                    banks[:, par, :].rearrange("p (b n) -> p b n", b=2),
                                    bias[:, 4 * a + par:4 * a + par + 3:2, 2 - 2 * t:6 - 2 * t, :].rearrange(
                                        "p b i n -> p b (i n)"), ALU.add).then_inc(s["biased"], 1)
                            dve.wait_ge(s["biased"], 2 * u + 2)
                            src = sc[:, u % 2]
                        else:
                            src = banks.rearrange("p b (c n) -> p (b c) n", c=2)
                        dve.tensor_reduce(nmax[:, u % 2, :], src, AX.X, ALU.max, negate=True
                                          ).then_inc(s["max_ready"], 1)
                    if 1 <= u <= units:
                        half = (u - 1) % 2
                        dve.wait_ge(s["exp_ready"], u)
                        link(dve.reciprocal(rsums[:, half, :], psums[:, half, :]))
                        for q in range(4):
                            last = dve.tensor_scalar(sc[:, half, q, :], sc[:, half, q, :], rsums[:, half, q:q + 1],
                                                     None, ALU.mult)
                        last.then_inc(s["probs_ready"], 1)
                    if u >= 3:
                        dve.wait_ge(s["o_hi_ready"], u - 2)
                        lo, src = outputs(i, u - 3, act_lo)
                        hi, _ = outputs(i, u - 3, act_hi.bitcast(F32))
                        dve.tensor_tensor(lo, src, hi, ALU.subtract).then_inc(s["o_split"], 1)

            def rotate_heads(t):
                qk = qkv[:, t, 0:NORM_HEADS * HD]
                heads = qk.rearrange("p (n d) -> p n d", d=HD)
                dve.wait_ge(qkv_kept[1], t + 1)
                if t > 0:
                    dve.wait_ge(heads_turned, t)
                link(dve.tensor_tensor(rot_a[:], qk, qk, ALU.mult))
                link(dve.tensor_reduce(head_rs[:], rot_a[:].rearrange("p (n d) -> p n d", d=HD), AX.X, ALU.add))
                dve.tensor_scalar(head_ms[:], head_rs[:], 1.0 / HD, EPS, ALU.mult, ALU.add).then_inc(heads_ms, 1)
                dve.wait_ge(heads_std, t + 1)
                link(dve.reciprocal(head_rs[:], head_std[:]))
                link(dve.tensor_scalar(head_rs[:, 0:HEADS], head_rs[:, 0:HEADS], HD ** -0.5, None, ALU.mult))
                link(dve.tensor_tensor(heads, heads, head_rs[:].unsqueeze(2).to_broadcast([P, NORM_HEADS, HD]),
                                       ALU.mult))
                for g in range(2):
                    cos = cst[:, C_COS + t * HD:C_COS + (t + 1) * HD]
                    sin = cst[:, C_SIN + t * HD:C_SIN + (t + 1) * HD].rearrange("p (a b f) -> p a b f", a=2, b=2)
                    swapped = qk_sin[:, g, :].rearrange("p (a b f) -> p a b f", a=2, b=2)
                    other = qk_gain[:, g, :].rearrange("p (a b f) -> p a b f", a=2, b=2)
                    link(dve.tensor_tensor(qk_cos[:, g, :], cos, qk_gain[:, g, :], ALU.mult))
                    for b in range(2):
                        link(dve.tensor_tensor(swapped[:, :, b, :], sin[:, :, b, :], other[:, :, 1 - b, :], ALU.mult))
                for g, (n0, n) in enumerate(((0, HEADS), (HEADS, KV_HEADS))):
                    own = heads[:, n0:n0 + n, :]
                    ra = rot_a[:, n0 * HD:(n0 + n) * HD].rearrange("p (n d) -> p n d", d=HD)
                    link(dve.tensor_tensor(ra, own, qk_cos[:, g, :].unsqueeze(1).to_broadcast([P, n, HD]), ALU.mult))
                    for axis in range(2):
                        for b in range(2):
                            d0, s0 = axis * 32 + b * 16, axis * 32 + (1 - b) * 16
                            rb = rot_b[:, n0 * HD:(n0 + n) * HD].rearrange("p (n d) -> p n d", d=HD)
                            link(dve.tensor_tensor(
                                rb[:, :, d0:d0 + 16], own[:, :, s0:s0 + 16],
                                qk_sin[:, g, d0:d0 + 16].unsqueeze(1).to_broadcast([P, n, 16]), ALU.mult))
                link(dve.tensor_tensor(qkv[:, t, 0:NQ], rot_a[:, 0:NQ], rot_b[:, 0:NQ], ALU.add))
                for copy in range(2):
                    last = dve.tensor_tensor(kdup[:, :, copy, :],
                                             rot_a[:, NQ:NQ + NKV].rearrange("p (n d) -> p n d", d=HD),
                                             rot_b[:, NQ:NQ + NKV].rearrange("p (n d) -> p n d", d=HD), ALU.add)
                    last.then_inc(heads_ready, 1)

            dve.wait_ge(x_in, 16)
            pre_norm(0, 0)
            split_until(O0 + SPLIT)
            dve.wait_ge(bias_masked, 4)
            attention(0)
            split_until(F0)
            post_norm(1, from_banks(0))
            split_until(F0 + SPLIT)
            pre_norm(2, 4)
            for s in range(STEPS):
                last = first_piece(s) + 3
                split_until(F0 + last + 3)
                dve.wait_ge(f0["silu"], s + 1)
                dve.tensor_tensor(hid[:], sil[:], ps[:, 1:4:2, :], ALU.mult).then_inc(f0["hid"], 1)
                if s > 0:
                    split_until(F0 + min(last + 4, FFN_PIECES))
                dve.wait_ge(f0["hT_hi"], s + 1)
                dve.tensor_tensor(hT_lo[:, s % 2], ps[:, 0:4:2, :], hT_hi[:, s % 2].bitcast(F32), ALU.subtract
                                  ).then_inc(f0["hT"], 1)
            split_until(Q1)
            post_norm(3, from_banks(4))
            split_until(Q1 + SPLIT)
            pre_norm(4, 0)
            split_until(O1)
            dve.wait_ge(qk_gain_in, 32)
            for t in range(T):
                rotate_heads(t)
            split_until(O1 + SPLIT)
            attention(1)
            split_until(J0)
            post_norm(5, from_banks(0))
            split_until(J0 + SPLIT)
            pre_norm(6, 4)
            for t in range(T):
                dve.wait_ge(tok_hi_ready, t + 1)
                dve.tensor_tensor(tok_lo[:, t, :], nrm[:, t, :], tok_hi[:, t, :].bitcast(F32), ALU.subtract
                                  ).then_inc(tok_ready, 1)

            def over_pairs(ap):
                return (ap.unsqueeze(2).to_broadcast([P, T, E, E]), ap.unsqueeze(3).to_broadcast([P, T, E, E]))

            dve.wait_ge(logits_ready, 1)
            link(dve.tensor_copy(logit[:], ps[:, 0, 0:T * E].rearrange("p (t e) -> p t e", t=T)))
            dve.tensor_reduce(r1[:, 0:T], logit[:], AX.X, ALU.max, negate=True).then_inc(logits_kept, 1)
            tri = cst[:, C_TRI:C_TRI + E * E].rearrange("p (e j) -> p e j", e=E)
            for t in range(T):
                lj = logit[:, t, :].unsqueeze(1).to_broadcast([P, E, E])
                le = logit[:, t, :].unsqueeze(2).to_broadcast([P, E, E])
                link(dve.tensor_tensor(pair[:, t], lj, le, ALU.is_gt))
                link(dve.tensor_tensor(pair2[:, t], lj, le, ALU.is_equal))
                link(dve.tensor_tensor(pair2[:, t], pair2[:, t], tri, ALU.mult))
            link(dve.tensor_tensor(pair[:], pair[:], pair2[:], ALU.add))
            link(dve.tensor_reduce(prod8[:], pair[:], AX.X, ALU.add))
            dve.tensor_scalar(chosen[:], prod8[:], float(TOP_K), None, ALU.is_lt).then_inc(chosen_ready, 1)
            dve.wait_ge(chosen_ready, 1)
            dve.wait_ge(logits_exp, T)
            link(dve.tensor_tensor(gate[:], gate[:], chosen[:], ALU.mult))
            link(dve.tensor_reduce(r1[:, 2:2 + T], gate[:], AX.X, ALU.add))
            link(dve.reciprocal(r1[:, 4:4 + T], r1[:, 2:2 + T]))
            for t in range(T):
                link(dve.tensor_scalar(gate[:, t, :], gate[:, t, :], r1[:, 4 + t:5 + t], None, ALU.mult))
            dve.wait_ge(pos_ready, 1)
            link(dve.tensor_scalar(pos[:], ps[:, 1, 0:T * E].rearrange("p (t e) -> p t e", t=T), 1.0, None, ALU.add))
            link(dve.tensor_tensor(pos[:], pos[:], chosen[:], ALU.mult))
            link(dve.tensor_scalar(pos[:], pos[:], -1.0, None, ALU.add))
            link(dve.memset(job_pos[:], -1.0))
            link(dve.memset(job_gate[:], 0.0))
            link(dve.tensor_copy(job_pos[:, :, 0:E], pos[:]))
            link(dve.tensor_copy(job_gate[:, :, 0:E], gate[:]))
            full, before, mine = r8[:, 0, :], r8[:, 1, :], r8[:, 2, :]
            link(dve.tensor_scalar(full, ps[:, 1, T * E:(T + 1) * E], float(P), None, ALU.is_gt))
            link(dve.tensor_tensor(pair[:, 0], full.unsqueeze(1).to_broadcast([P, E, E]), tri, ALU.mult))
            link(dve.tensor_reduce(before, pair[:, 0], AX.X, ALU.add))
            link(dve.tensor_reduce(over_f[:, 0:1], full, AX.X, ALU.add))
            far = 1000.0
            link(dve.tensor_scalar(pos[:], pos[:], far - P, None, ALU.add))
            for i in range(MAX_OVER):
                link(dve.tensor_scalar(mine, before, float(i), None, ALU.is_equal))
                link(dve.tensor_tensor(mine, mine, full, ALU.mult))
                link(dve.tensor_tensor(r8[:, 3, :], mine, cst[:, C_EXP:C_EXP + E], ALU.mult))
                link(dve.tensor_reduce(over_f[:, 1 + i:2 + i], r8[:, 3, :], AX.X, ALU.add))
                for src, dst in ((pos, job_pos), (gate, job_gate)):
                    link(dve.tensor_tensor(prod8[:], src[:], mine.unsqueeze(1).to_broadcast([P, T, E]), ALU.mult))
                    link(dve.tensor_reduce(dst[:, :, E + i:E + i + 1], prod8[:], AX.X, ALU.add))
            link(dve.tensor_scalar(job_pos[:, :, E:E + MAX_OVER], job_pos[:, :, E:E + MAX_OVER], -far, None, ALU.add))
            dve.tensor_copy(over[:], over_f[:]).then_inc(over_ready, 1)

            def build_pick(j):
                if not isinstance(j, int) or j > 0:
                    dve.wait_ge(pick_turned, j)
                column = bass.ds(j, 1)
                dve.tensor_copy(cur[:, 0, :].unsqueeze(2), job_pos[:, :, column]).then_inc(cur_ready, 1)
                dve.tensor_copy(cur[:, 1, :].unsqueeze(2), job_gate[:, :, column]).then_inc(cur_ready, 1)
                dve.wait_ge(cur_ready, 2 * j + 2)
                iota = cst[:, C_IOTA:C_IOTA + P]
                for t in range(T):
                    dve.tensor_scalar(pick[:, t, :], iota, cur[:, 0, t:t + 1], None, ALU.is_equal
                                      ).then_inc(pick_ready, 1)
                    dve.tensor_scalar(pick_g[:, t, :], iota, cur[:, 0, t:t + 1], cur[:, 1, t:t + 1],
                                      ALU.is_equal, ALU.mult).then_inc(pick_ready, 1)

            def keep_gathered(j):
                dve.wait_ge(x_hi_ready, j + 1)
                dve.tensor_tensor(act_lo[:, :, 0:P], ps[:, 6:8, :].rearrange("p b (c n) -> p (b c) n", c=4),
                                  act_hi[:, :, 0:P].bitcast(F32), ALU.subtract).then_inc(x_ready, 1)

            def add_outputs(j):
                dve.wait_ge(scattered, j + 1)
                for t, b in enumerate((4, 2)):
                    dve.tensor_tensor(nrm[:, t, :], nrm[:, t, :],
                                      ps[:, b:b + 2, :].rearrange("p b n -> p (b n)"), ALU.add).then_inc(y_added, 1)

            def expert_job(j):
                first = isinstance(j, int)
                split_at[0] = J0 + SPLIT if first else J0
                split_until(J0 + SPLIT, j)
                if not first:
                    dve.wait_ge(y_added, T * j)
                    add_outputs(j - 1)
                for s in range(STEPS):
                    split_until(J0 + 6 * s + (4 if s else 6), j)
                    dve.wait_ge(fj["silu"], j * STEPS + s + 1)
                    dve.tensor_tensor(hid[:, 0, :], sil[:, 0, :], ps[:, 2 * (s % 2) + 1, :], ALU.mult
                                      ).then_inc(fj["hid"], 1)
                    if s == STEPS - 1:
                        build_pick(j + 1)
                    split_until(J0 + min(6 * s + 8, FFN_PIECES), j)
                    dve.wait_ge(fj["hT_hi"], j * STEPS + s + 1)
                    dve.tensor_tensor(hT_lo[:, 0, 0, :], ps[:, 2 * (s % 2), :], hT_hi[:, 0, 0, :].bitcast(F32),
                                      ALU.subtract).then_inc(fj["hT"], 1)
                keep_gathered(j + 1)

            build_pick(0)
            dve.wait_ge(nrm_turned, 16)
            dve.wait_ge(tok_ready, T)
            for t in range(T):
                dve.memset(nrm[:, t, :], 0.0).then_inc(y_added, 1)
            keep_gathered(0)
            expert_job(0)
            with dve.Fori(1, E) as j:
                expert_job(j)
            n_over = dve.value_load(over[0:1, 0:1], min_val=0, max_val=MAX_OVER)
            with dve.If(n_over > 0):
                with dve.Fori(0, n_over) as i:
                    expert_job(i + E)
            dve.wait_ge(y_added, (n_over + E) * T)
            add_outputs(n_over + (E - 1))
            post_norm(7, lambda t: nrm[:, t, :])

        @block.tensor
        def _(pe):
            def product(out, hi, lo, slot, b, start, stop):
                wh, wl = w_hi[:, slot, b, :], w_lo[:, slot, b, :]
                pe.matmul(out, hi, wh, start=start, stop=False)
                pe.matmul(out, hi, wl, start=False, stop=False)
                return pe.matmul(out, lo, wh, start=False, stop=stop)

            def take(n, job=None):
                pe.wait_ge(lo_ready, (0 if job is None else job * FFN_PIECES) + n + 1)

            def turn_norm(k, bank):
                if k == 0:
                    pe.wait_ge(cst_in, 16)
                for t in range(T):
                    pe.wait_ge(nrm_ready, T * (k // 2) + t + 1)
                    for c in range(KC):
                        ins = pe.transpose(ps[:, bank + 2 * t + c // 4, (c % 4) * P:(c % 4 + 1) * P],
                                           nrm[:, t, c * P:(c + 1) * P], ident)
                        if c % 4 == 3:
                            ins.then_inc(nrm_turned, 1)

            def token_product(n0, chunks, banks):
                for j in range(chunks):
                    for half in range(2):
                        n = n0 + 2 * j + half
                        take(n)
                        for b in range(PK):
                            c = PK * half + b
                            for t in range(T):
                                tok = slice(t * P, (t + 1) * P)
                                last = product(ps[:, banks(t, j), :], act_hi[:, c, tok], act_lo[:, c, tok],
                                               n % SPLIT, b, c == 0, c == KC - 1)
                        last.then_inc(piece_used, 1)
                return last

            def attention(i, kv_chunk, value):
                s = att[i]
                units = 2 * HEADS // 4
                for u in range(units + 2):
                    if u < units:
                        a, t = u // 2, u % 2
                        if u >= 2:
                            if i == 0:
                                pe.wait_ge(s["biased"], 2 * (u - 1))
                            else:
                                pe.wait_ge(s["exp_ready"], u - 1)
                        for b in range(2):
                            for par in range(2):
                                head = 4 * a + 2 * b + par
                                rows = slice(par * HD, (par + 1) * HD)
                                last = pe.matmul(ps[:, 2 * (u % 2) + par, b * SEQ:(b + 1) * SEQ],
                                                 qT[rows, head // 2, t * P:(t + 1) * P],
                                                 kT[rows, kv_chunk(head), :], start=True, stop=True)
                        last.then_inc(s["scores_ready"], 1)
                    if 1 <= u <= units:
                        pe.wait_ge(s["probs_ready"], u)
                        if u >= 2:
                            pe.wait_ge(s["pT_ready"], u - 1)
                        for q in range(4):
                            for c in range(2):
                                m = 2 * (q % 2) + c
                                last = pe.transpose(ps[:, 4 + q // 2, m * P:(m + 1) * P],
                                                    sc[:, (u - 1) % 2, q, c * P:(c + 1) * P], ident)
                        last.then_inc(s["probs_turned"], 1)
                    if u >= 2:
                        w = u - 2
                        pe.wait_ge(s["pT_ready"], w + 1)
                        if w >= 2:
                            pe.wait_ge(s["o_split"], w - 1)
                        for q in range(4):
                            par, b = q // 2, q % 2
                            head = 4 * (w // 2) + 2 * b + par
                            for c in range(2):
                                last = pe.matmul(ps[par * HD:(par + 1) * HD, 6 + w % 2, b * P:(b + 1) * P],
                                                 value(c, head), pT[:, w % 2, 2 * q + c, :],
                                                 start=(c == 0), stop=(c == 1))
                        last.then_inc(s["o_ready"], 1)

            def down(n, job, y_banks, s, half, buf, tiles):
                take(n, job)
                for b in range(PK):
                    for t in range(tiles):
                        last = product(ps[:, y_banks(t) + half, :], hT_hi[:, buf, t, b * P:(b + 1) * P],
                                       hT_lo[:, buf, t, b * P:(b + 1) * P], n % SPLIT, b,
                                       s == 0 and b == 0, s == STEPS - 1 and b == PK - 1)
                last.then_inc(piece_used, 1)
                return last

            turn_norm(0, 0)
            pe.wait_ge(act_ready, 2 * T)
            for j in range(4):
                if j >= 2:
                    pe.wait_ge(qkv_kept[0], j - 1)
                for half in range(2):
                    n = Q0 + 2 * j + half
                    take(n)
                    for b in range(PK):
                        c = PK * half + b
                        for m in range(4):
                            o = ps[:, 4 * (j % 2) + m, 0:SEQ]
                            wh = w_hi[:, n % SPLIT, b, m * P:(m + 1) * P]
                            wl = w_lo[:, n % SPLIT, b, m * P:(m + 1) * P]
                            pe.matmul(o, wh, act_hi[:, c, :], start=(c == 0), stop=False)
                            pe.matmul(o, wh, act_lo[:, c, :], start=False, stop=False)
                            last = pe.matmul(o, wl, act_hi[:, c, :], start=False, stop=(c == KC - 1))
                    last.then_inc(piece_used, 1)
                pe.wait_ge(piece_used, Q0 + 2 * j + 2)
                pe.sem_inc(qkv_ready[0], 1)
            for j in range(4, 6):
                pe.wait_ge(qkv_kept[0], j - 1)
                token_product(Q0 + 2 * j, 1, lambda t, _: 4 * (j % 2) + t)
                pe.wait_ge(piece_used, Q0 + 2 * j + 2)
                pe.sem_inc(qkv_ready[0], 1)
            pe.wait_ge(qkv_kept[0], 6)
            attention(0, lambda head: head // 2, lambda c, head: v0[:, c, head * HD:(head + 1) * HD])
            pe.wait_ge(att[0]["o_split"], 8)
            token_product(O0, 2, lambda t, j: 2 * t + j)
            pe.wait_ge(piece_used, F0)
            pe.sem_inc(proj_ready, 1)

            turn_norm(2, 4)
            pe.wait_ge(act_ready, 4 * T)
            for s in range(STEPS):
                n = F0 + first_piece(s)
                if s >= 1:
                    pe.wait_ge(f0["hT"], s)
                for m in range(4):
                    take(n + m)
                    for b in range(PK):
                        c = PK * (m % 2) + b
                        for t in range(T):
                            tok = slice(t * P, (t + 1) * P)
                            last = product(ps[:, 2 * t + m // 2, :], act_hi[:, c, tok], act_lo[:, c, tok],
                                           (n + m) % SPLIT, b, c == 0, c == KC - 1)
                    last.then_inc(piece_used, 1)
                pe.wait_ge(piece_used, n + 4)
                pe.sem_inc(f0["gu"], 1)
                if s >= 1:
                    down(n + 4, None, lambda t: 4 + 2 * t, s - 1, 0, (s - 1) % 2, T)
                pe.wait_ge(f0["hid"], s + 1)
                for t in range(T):
                    for b in range(PK):
                        last = pe.transpose(ps[:, 2 * t, b * P:(b + 1) * P], hid[:, t, b * P:(b + 1) * P], ident)
                last.then_inc(f0["turned"], 1)
                if s >= 1:
                    down(n + 5, None, lambda t: 4 + 2 * t, s - 1, 1, (s - 1) % 2, T)
            pe.wait_ge(f0["hT"], STEPS)
            for half in range(2):
                down(Q1 - 2 + half, None, lambda t: 4 + 2 * t, STEPS - 1, half, (STEPS - 1) % 2, T)
            pe.wait_ge(piece_used, Q1)
            pe.sem_inc(f0["y"], 1)

            turn_norm(4, 0)
            pe.wait_ge(act_ready, 6 * T)
            token_product(Q1, QKV1 // COLS, lambda t, j: 2 * j + t)
            pe.wait_ge(piece_used, O1)
            pe.sem_inc(qkv_ready[1], 1)
            pe.wait_ge(qkv_kept[1], T)
            for t in range(T):
                pe.wait_ge(heads_ready, 2 * t + 2)
                if t > 0:
                    pe.wait_ge(heads_kept, 2 * t)
                for c in range(KC):
                    pe.transpose(ps[:, c // 4, (c % 4) * P:(c % 4 + 1) * P], qkv[:, t, c * P:(c + 1) * P], ident)
                for g in range(KV_HEADS):
                    last = pe.transpose(ps[:, 2, g * P:(g + 1) * P], kdup[:, g].rearrange("p a d -> p (a d)"), ident)
                last.then_inc(heads_turned, 1)
            pe.wait_ge(heads_kept, 2 * T)
            v_at = NQ + NKV
            attention(1, lambda head: head // 4,
                      lambda c, head: qkv[:, c, v_at + (head // 4) * HD:v_at + (head // 4 + 1) * HD])
            pe.wait_ge(att[1]["o_split"], 8)
            token_product(O1, 2, lambda t, j: 2 * t + j)
            pe.wait_ge(piece_used, J0)
            pe.sem_inc(proj_ready, 1)

            turn_norm(6, 4)
            pe.wait_ge(wr_in, 16)
            pe.wait_ge(fT_ready, 2 * T)
            for t in range(T):
                for c in range(KC):
                    last = pe.matmul(ps[:, 0, t * E:(t + 1) * E], fT[:, c, t * P:(t + 1) * P], wr[:, c, :],
                                     start=(c == 0), stop=(c == KC - 1))
            last.then_inc(logits_ready, 1)
            pe.wait_ge(chosen_ready, 1)
            before, ones = cst[:, C_BEFORE:C_BEFORE + P], cst[:, C_ONES:C_ONES + P]
            pe.matmul(ps[:, 1, 0:E], before, chosen[:, 0, :], start=True, stop=True)
            pe.matmul(ps[:, 1, E:2 * E], ones, chosen[:, 0, :], start=True, stop=False)
            pe.matmul(ps[:, 1, E:2 * E], before, chosen[:, 1, :], start=False, stop=True)
            pe.matmul(ps[:, 1, 2 * E:3 * E], ones, chosen[:, 0, :], start=True, stop=False)
            pe.matmul(ps[:, 1, 2 * E:3 * E], ones, chosen[:, 1, :], start=False, stop=True).then_inc(pos_ready, 1)

            def gather(j):
                pe.wait_ge(pick_ready, 4 * j + 4)
                for c in range(KC):
                    o = ps[:, 6 + c // 4, (c % 4) * P:(c % 4 + 1) * P]
                    for t in range(T):
                        pe.matmul(o, tok_hi[:, t, c * P:(c + 1) * P], pick[:, t, :], start=(t == 0), stop=False)
                        last = pe.matmul(o, tok_lo[:, t, c * P:(c + 1) * P], pick[:, t, :], start=False,
                                         stop=(t == T - 1))
                last.then_inc(gathered, 1)

            def turn_pick():
                for t in range(T):
                    last = pe.transpose(ps[:, 1, t * P:(t + 1) * P], pick_g[:, t, :], ident)
                last.then_inc(pick_turned, 1)

            def expert_job(j):
                pe.wait_ge(x_ready, j + 1)
                for s in range(STEPS):
                    n = J0 + first_piece(s)
                    q = 2 * (s % 2)
                    if s == 1:
                        pe.wait_ge(y_added, T * j + T)
                    for m in range(4):
                        if s == 0 and m == 2:
                            pe.wait_ge(pickT_ready, j + 1)
                        take(n + m, j)
                        for b in range(PK):
                            c = PK * (m % 2) + b
                            last = product(ps[:, q + m // 2, :], act_hi[:, c, 0:P], act_lo[:, c, 0:P],
                                           (n + m) % SPLIT, b, c == 0, c == KC - 1)
                        last.then_inc(piece_used, 1)
                        if m == 1 and s >= 1:
                            turn_hidden(j, s - 1)
                    pe.wait_ge(piece_used, j * FFN_PIECES + n + 4)
                    pe.sem_inc(fj["gu"], 1)
                    if s >= 1:
                        pe.wait_ge(fj["hT"], j * STEPS + s)
                        for half in range(2):
                            down(n + 4 + half, j, lambda t: 4, s - 1, half, 0, 1)
                turn_hidden(j, STEPS - 1)
                gather(j + 1)
                pe.wait_ge(fj["hT"], j * STEPS + STEPS)
                for half in range(2):
                    last = down(J0 + FFN_PIECES - 2 + half, j, lambda t: 4, STEPS - 1, half, 0, 1)
                pe.wait_ge(piece_used, j * FFN_PIECES + J0 + FFN_PIECES)
                pe.sem_inc(fj["y"], 1)
                pe.wait_ge(y_kept, j + 1)
                for t, bank in enumerate((4, 2)):
                    for half in range(2):
                        last = pe.matmul(ps[:, bank + half, :], pick_gT[:, t, :],
                                         y_sb[:, half * COLS:(half + 1) * COLS], start=True, stop=True)
                last.then_inc(scattered, 1)
                turn_pick()

            def turn_hidden(j, s):
                pe.wait_ge(fj["hid"], j * STEPS + s + 1)
                for b in range(PK):
                    last = pe.transpose(ps[:, 2 * (s % 2), b * P:(b + 1) * P], hid[:, 0, b * P:(b + 1) * P], ident)
                last.then_inc(fj["turned"], 1)

            pe.wait_ge(tok_ready, T)
            pe.wait_ge(over_ready, 1)
            gather(0)
            turn_pick()
            expert_job(0)
            with pe.Fori(1, E) as j:
                expert_job(j)
            n_over = pe.value_load(over[0:1, 0:1], min_val=0, max_val=MAX_OVER)
            with pe.If(n_over > 0):
                with pe.Fori(0, n_over) as i:
                    expert_job(i + E)


_INS = ["x", "norm_g", "na_w_qkv", "na_rpb", "na_w_o", "gqa_w_qkv", "gqa_q_norm", "gqa_k_norm", "gqa_w_o",
        "ffn_w_gate", "ffn_w_up", "ffn_w_down", "moe_w_router", "moe_w_gate", "moe_w_up", "moe_w_down"]


def kernel(**inputs):
    import concourse.bacc as bacc
    from concourse.bass_utils import run_bass_kernel_spmd

    nc = bacc.Bacc("TRN2", target_bir_lowering=False, num_devices=1)
    arrays, args = {}, []
    for name in _INS:
        a = np.ascontiguousarray(inputs[name])
        arrays[f"in_{name}"] = a
        args.append(nc.dram_tensor(f"in_{name}", a.shape, mybir.dt.from_np(a.dtype), kind="ExternalInput").ap())
    arrays["in_consts"] = constants()
    args.append(nc.dram_tensor("in_consts", (P, C_ALL), F32, kind="ExternalInput").ap())
    args.append(nc.dram_tensor("out_0", (1, SEQ, D), F32, kind="ExternalOutput").ap())
    encoder_kernel(nc, *args)
    r = run_bass_kernel_spmd(nc, [arrays], core_ids=[0])
    return r.results[0]["out_0"]
```

```python
from contextlib import ExitStack

import numpy as np

import concourse.bass as bass
from concourse import mybir

F32 = mybir.dt.float32
F32R = mybir.dt.float32r
I32 = mybir.dt.int32
ACT = mybir.ActivationFunctionType
ALU = mybir.AluOpType
AX = mybir.AxisListType

P = 128
D = 1024
SEQ = 256
T = SEQ // P
KC = D // P
GRID_W = 64
ROWS = SEQ // GRID_W
HEADS = 16
HD = 64
KV_HEADS = 4
WIN_H, WIN_W = 8, 16
RPB_H, RPB_W = 2 * WIN_H - 1, 2 * WIN_W - 1
D_FF = D * 7 // 2
E = 8
TOP_K = 2
EPS = 1e-6
NQ = HEADS * HD
NKV = KV_HEADS * HD
QKV1 = NQ + 2 * NKV
NORM_HEADS = HEADS + KV_HEADS
MASKED = -1e30

COLS = 512
PK = 4
RAW = 6
SPLIT = 3
STEPS = D_FF // COLS
FFN_PIECES = 6 * STEPS

Q0 = 0
O0 = Q0 + 2 * (3 * D // COLS)
F0 = O0 + 2 * (D // COLS)
Q1 = F0 + FFN_PIECES
O1 = Q1 + 2 * (QKV1 // COLS)
J0 = O1 + 2 * (D // COLS)

MAX_OVER = TOP_K * SEQ // (P + 1)
JOB_COLS = E + MAX_OVER + 1

C_IDENT, C_IOTA, C_BEFORE, C_ONES = 0, P, 2 * P, 3 * P
C_TRI = 4 * P
C_EXP = C_TRI + E * E
C_COS = C_EXP + E
C_SIN = C_COS + T * HD
C_ALL = C_SIN + T * HD


def constants():
    c = np.zeros((P, C_ALL), np.float32)
    c[:, C_IDENT:C_IDENT + P] = np.eye(P)
    c[:, C_IOTA:C_IOTA + P] = np.arange(P)
    c[:, C_BEFORE:C_BEFORE + P] = np.triu(np.ones((P, P)), 1)
    c[:, C_ONES:C_ONES + P] = 1.0
    c[:, C_TRI:C_TRI + E * E] = np.tril(np.ones((E, E)), -1).reshape(1, -1)
    c[:, C_EXP:C_EXP + E] = np.arange(E)
    quarter = HD // 4
    freqs = (np.float32(10000.0) ** (-np.arange(quarter, dtype=np.float32) / np.float32(quarter))).astype(np.float32)
    for t in range(T):
        tok = t * P + np.arange(P)
        for axis, pos in enumerate((tok // GRID_W, tok % GRID_W)):
            ang = pos.astype(np.float32)[:, None] * freqs[None, :]
            a = axis * HD // 2
            cos, sin = C_COS + t * HD + a, C_SIN + t * HD + a
            c[:, cos:cos + quarter] = c[:, cos + quarter:cos + 2 * quarter] = np.cos(ang)
            c[:, sin:sin + quarter] = -np.sin(ang)
            c[:, sin + quarter:sin + 2 * quarter] = np.sin(ang)
    return c


def first_piece(s):
    return 0 if s == 0 else 4 + 6 * (s - 1)


def encoder_kernel(nc, x, norm_g, na_w_qkv, na_rpb, na_w_o, gqa_w_qkv, gqa_q_norm, gqa_k_norm, gqa_w_o,
                   ffn_w_gate, ffn_w_up, ffn_w_down, moe_w_router, moe_w_gate, moe_w_up, moe_w_down,
                   consts, out):
    ctx = ExitStack()
    with ctx:
        def sb(name, shape, dt=F32, scope=None):
            return (scope or ctx).enter_context(nc.sbuf_tensor(name, shape, dt))

        def sem(name):
            return ctx.enter_context(nc.semaphore(name))

        raw = sb("raw", [P, RAW, PK, COLS])
        w_hi = sb("w_hi", [P, SPLIT, PK, COLS], F32R)
        w_lo = sb("w_lo", [P, SPLIT, PK, COLS], F32R)
        h = sb("h", [P, T, D])
        nrm = sb("nrm", [P, T, D])
        act_hi = sb("act_hi", [P, KC, SEQ], F32R)
        act_lo = sb("act_lo", [P, KC, SEQ], F32R)
        gain = sb("gain", [P, 2, D])
        cst = sb("cst", [P, C_ALL])
        wr = sb("wr", [P, KC, E])
        small = sb("small", [P, 64])
        junk = sb("junk", [P, D], mybir.dt.bfloat16)
        ident = cst[:, C_IDENT:C_IDENT + P]
        sumsq = small[:, 40:44].rearrange("p (t j) -> p t j", t=T)
        part, meansq, std, rstd = (small[:, 4 * i:4 * i + 2] for i in range(4))
        nmax = small[:, 16:24].rearrange("p (b s) -> p b s", b=2)
        psums = small[:, 24:32].rearrange("p (b s) -> p b s", b=2)
        pmax = small[:, 48:56].rearrange("p (b s) -> p b s", b=2)
        rsums = small[:, 32:40].rearrange("p (b s) -> p b s", b=2)
        attn = ExitStack()
        qT = sb("qT", [P, KC, SEQ], F32, attn)
        kT = sb("kT", [P, KC, SEQ], F32, attn)
        sc = sb("sc", [P, 2, 4, SEQ], F32, attn)
        pT = sb("pT", [P, 2, 8, P], F32, attn)
        layer0 = ExitStack()
        v0 = sb("v0", [P, T, D], F32, layer0)
        bias = sb("bias", [P, HEADS, ROWS + 2, GRID_W], F32, layer0)
        layer0.close()
        layer1 = ExitStack()
        qkv = sb("qkv", [P, T, QKV1], F32, layer1)
        rot_a = sb("rot_a", [P, T, COLS], F32, layer1)
        rot_b = sb("rot_b", [P, T, COLS], F32, layer1)
        kdup = sb("kdup", [P, T, KV_HEADS, 2, HD], F32, layer1)
        qk_gain = sb("qk_gain", [P, 2, HD], F32, layer1)
        qk_cos = sb("qk_cos", [P, 2, T, HD], F32, layer1)
        qk_sin = sb("qk_sin", [P, 2, T, HD], F32, layer1)
        head_ss = sb("head_ss", [P, 3, T, 8], F32, layer1)
        head_ms = sb("head_ms", [P, 3, T, 8], F32, layer1)
        head_std = sb("head_std", [P, 3, T, 8], F32, layer1)
        head_rs = sb("head_rs", [P, 3, T, 8], F32, layer1)
        layer1.close()
        attn.close()
        ffn = ExitStack()
        hid = sb("hid", [P, T, COLS], F32, ffn)
        sil = sb("sil", [P, T, COLS], F32, ffn)
        hT_hi = sb("hT_hi", [P, 2, T, PK * P], F32R, ffn)
        hT_lo = sb("hT_lo", [P, 2, T, PK * P], F32R, ffn)
        tok_hi = sb("tok_hi", [P, T, D], F32R, ffn)
        tok_lo = sb("tok_lo", [P, T, D], F32R, ffn)
        y_sb = sb("y_sb", [P, D], F32, ffn)
        fT = sb("fT", [P, KC, SEQ], F32, ffn)
        pick = sb("pick", [P, T, P], F32R, ffn)
        pick_g = sb("pick_g", [P, T, P], F32, ffn)
        pick_gT = sb("pick_gT", [P, T, P], F32, ffn)
        logit = sb("logit", [P, T, E], F32, ffn)
        pair = sb("pair", [P, T, E, E], F32, ffn)
        pair2 = sb("pair2", [P, T, E, E], F32, ffn)
        chosen = sb("chosen", [P, T, E], F32, ffn)
        gate = sb("gate", [P, T, E], F32, ffn)
        pos = sb("pos", [P, T, E], F32, ffn)
        r8 = sb("r8", [P, 6, E], F32, ffn)
        r1 = sb("r1", [P, 16], F32, ffn)
        prod8 = sb("prod8", [P, T, E], F32, ffn)
        job_pos = sb("job_pos", [P, T, JOB_COLS], F32, ffn)
        job_gate = sb("job_gate", [P, T, JOB_COLS], F32, ffn)
        cur = sb("cur", [P, 2, T], F32, ffn)
        over_f = sb("over_f", [P, 1 + MAX_OVER], F32, ffn)
        over = sb("over", [P, 1 + MAX_OVER], I32, ffn)
        ffn.close()
        ps = ctx.enter_context(nc.psum_tensor("ps", [P, 8, COLS], F32))

        landed = [sem(f"piece_landed_{i}") for i in range(RAW)]
        hi_ready, lo_ready, piece_used = sem("hi_ready"), sem("lo_ready"), sem("piece_used")
        x_in, cst_in, gain_in = [sem("x_in_0"), sem("x_in_1")], sem("cst_in"), [sem("gain_in_0"), sem("gain_in_1")]
        bias_in, bias_masked, qk_gain_in, wr_in = sem("bias_in"), sem("bias_masked"), sem("qk_gain_in"), sem("wr_in")
        gain_used = sem("gain_used")
        sumsq_ready, meansq_ready, std_ready = sem("sumsq_ready"), sem("meansq_ready"), sem("std_ready")
        nrm_ready, nrm_turned, act_hi_ready, act_ready = (
            sem("nrm_ready"), sem("nrm_turned"), sem("act_hi_ready"), sem("act_ready"))
        h_ready, tile0_done, scaled_ready = sem("h_ready"), sem("tile0_done"), sem("scaled_ready")
        dve_chain = sem("dve_chain")
        qkv_kept = [sem("qkv0_kept"), sem("qkv1_kept")]
        att = [{n: sem(f"{n}_{i}") for n in (
            "scores_ready", "biased", "max_ready", "exp_ready", "probs_ready", "probs_turned", "pT_ready",
            "o_ready", "o_hi_ready", "o_split")} for i in range(2)]
        heads_squared, heads_ms, heads_std, heads_ready, heads_turned, heads_kept = (
            sem("heads_squared"), sem("heads_ms"), sem("heads_std"), sem("heads_ready"), sem("heads_turned"),
            sem("heads_kept"))
        f0 = {n: sem(f"ffn_{n}") for n in ("silu", "hid", "turned", "hT_hi", "hT")}
        fj = {n: sem(f"job_{n}") for n in ("silu", "hid", "turned", "hT_hi", "hT")}
        tok_hi_ready, tok_ready, fT_ready, logits_ready = (
            sem("tok_hi_ready"), sem("tok_ready"), sem("fT_ready"), sem("logits_ready"))
        logits_kept, logits_exp, chosen_ready, pos_ready, over_ready = (
            sem("logits_kept"), sem("logits_exp"), sem("chosen_ready"), sem("pos_ready"), sem("over_ready"))
        cur_ready, pick_ready, gathered, x_hi_ready, x_ready = (
            sem("cur_ready"), sem("pick_ready"), sem("gathered"), sem("x_hi_ready"), sem("x_ready"))
        pick_turned, pickT_ready, y_kept, scattered, y_added = (
            sem("pick_turned"), sem("pickT_ready"), sem("y_kept"), sem("scattered"), sem("y_added"))
        out_stored = sem("out_stored")

        def rows_of(ap):
            return ap.rearrange("p b (r c) -> p b r c", c=GRID_W)[:, :, :, ::-1]

        def outputs(layer, u, acts):
            a, t = u // 2, u % 2
            dst = acts[:, 2 * a:2 * a + 2, t * P:(t + 1) * P]
            src = ps[:, 6 + u % 2, 0:2 * P].rearrange("p (b n) -> p b n", b=2)
            if layer == 0:
                return dst.rearrange("p b (r c) -> p b r c", c=GRID_W), rows_of(src)
            return dst, src

        def w_piece(w, k0, c0):
            return w[k0:k0 + PK * P, c0:c0 + COLS].rearrange("(b p) n -> p b n", p=P)

        def columns_then_halves(w, columns):
            return [(w, half * PK * P, c0) for c0 in columns for half in range(2)]

        qkv1_columns = (NQ, 0, COLS)

        def swiglu_pieces(w_gate, w_up, w_down):
            pieces = []
            for s in range(STEPS + 1):
                if s < STEPS:
                    for w in (w_gate, w_up):
                        pieces += [(w, half * PK * P, s * COLS) for half in range(2)]
                if s >= 1:
                    pieces += [(w_down, (s - 1) * COLS, half * COLS) for half in range(2)]
            return pieces

        front = (columns_then_halves(na_w_qkv[0], range(0, 3 * D, COLS)) + columns_then_halves(na_w_o[0], (0, COLS))
                 + swiglu_pieces(ffn_w_gate[0], ffn_w_up[0], ffn_w_down[0])
                 + columns_then_halves(gqa_w_qkv[0], qkv1_columns) + columns_then_halves(gqa_w_o[0], (0, COLS)))
        assert len(front) == J0 and FFN_PIECES % RAW == 0 and FFN_PIECES % SPLIT == 0

        PRODUCTS = {1: (O0, 0, F0), 3: (Q1 - 2, 4, Q1), 5: (O1, 0, J0)}
        TURN_BANK = {0: 0, 2: 4, 4: 0, 6: 4}

        SUMS = {(0, 0, 0): 1, (0, 1, 0): 2, (7, 0, 0): 21, (7, 1, 0): 22}
        ROOTS = {(0, 0): 1, (0, 1): 2, (7, 0): 15, (7, 1): 16}
        for k in PRODUCTS:
            first = [(k, 0, 0), (k, 0, 1), (k + 1, 0, 0), (k, 1, 0)] if k == 3 else [
                (k, 0, 0), (k, 1, 0), (k, 0, 1), (k + 1, 0, 0)]
            for i, key in enumerate(first + [(k, 1, 1), (k + 1, 1, 0)]):
                SUMS[key] = 2 + 6 * (k // 2) + i + 1
            for i, key in enumerate([(k, 0), (k + 1, 0), (k, 1), (k + 1, 1)]):
                ROOTS[key] = 2 + 4 * (k // 2) + i + 1

        def product_ready(k, t, j):
            n = PRODUCTS[k][0]
            if k == 3:
                return (tile0_done, 2 + j) if t == 0 else (piece_used, n + 1 + j)
            if j == 0:
                return piece_used, n + 2
            return (tile0_done, 1 if k == 1 else 4) if t == 0 else (piece_used, n + 4)

        block = ctx.enter_context(nc.Block())

        @block.sync
        def _(sp):
            def load(n, src, job=0):
                if not isinstance(n, int) or n >= RAW or not isinstance(job, int):
                    sp.wait_ge(lo_ready, job * FFN_PIECES + n - RAW + 1)
                sp.dma_start(raw[:, n % RAW, :, :], src).then_inc(landed[n % RAW], 16)

            def load_expert(job, expert):
                pieces = swiglu_pieces(moe_w_gate[0, expert], moe_w_up[0, expert], moe_w_down[0, expert])
                for i, piece in enumerate(pieces):
                    load(J0 + i, w_piece(*piece), job)

            for t in range(T):
                sp.dma_start(h[:, t, :], x[0, t * P:(t + 1) * P, :]).then_inc(x_in[t], 16)
            for n, piece in enumerate(front):
                load(n, w_piece(*piece))
            with sp.Fori(0, E) as e:
                load_expert(e, e)
            sp.wait_ge(over_ready, 1)
            n_over = sp.value_load(over[0:1, 0:1], min_val=0, max_val=MAX_OVER)
            with sp.If(n_over > 0):
                with sp.Fori(0, n_over) as i:
                    e = sp.value_load(over[0:1, bass.ds(i + 1, 1)], min_val=0, max_val=E - 1)
                    load_expert(i + E, e)
            for t in range(T):
                sp.wait_ge(h_ready, 4 * T - T + t + 1)
                sp.dma_start(out[0, t * P:(t + 1) * P, :], h[:, t, :]).then_inc(out_stored, 16)
            sp.wait_ge(out_stored, 16 * T)

        @block.gpsimd
        def _(pool):
            def load_gain(k):
                if k >= 2:
                    pool.wait_ge(gain_used, k - 1)
                g = norm_g[k // 4, k % 4:k % 4 + 1, :]
                pool.dma_start(gain[:, k % 2, :], g.to_broadcast([P, D])).then_inc(gain_in[k % 2], 16)

            pool.dma_start(cst[:], consts).then_inc(cst_in, 16)
            load_gain(0)
            load_gain(1)
            for a in range(2):
                for i in range(ROWS + 2):
                    src = bass.AP(na_rpb.tensor, (WIN_H - ROWS + 1 - a + i) * RPB_W + WIN_W - GRID_W,
                                  [[1, GRID_W], [RPB_H * RPB_W, HEADS], [1, GRID_W]])
                    pool.dma_start(bias[a * GRID_W:(a + 1) * GRID_W, :, i, :], src).then_inc(bias_in, 16)
            pool.wait_ge(bias_in, 2 * (ROWS + 2) * 16)
            edge = GRID_W - WIN_W
            for a in range(2):
                b = bias[a * GRID_W:(a + 1) * GRID_W].rearrange("p h i k -> p (h i) k")
                rows = HEADS * (ROWS + 2)
                pool.affine_select(out=b[:, :, 0:edge], in_=b[:, :, 0:edge], compare_op=ALU.is_ge, fill=MASKED,
                                   base=WIN_W // 2 - GRID_W + 1, pattern=[[0, rows], [1, edge]],
                                   channel_multiplier=1
                                   ).then_inc(bias_masked, 1)
                pool.wait_ge(bias_masked, 2 * a + 1)
                pool.affine_select(out=b[:, :, WIN_W:], in_=b[:, :, WIN_W:], compare_op=ALU.is_ge, fill=MASKED,
                                   base=WIN_W // 2 - 1 - WIN_W + GRID_W - 1, pattern=[[0, rows], [-1, edge]],
                                   channel_multiplier=-1).then_inc(bias_masked, 1)
            for k in range(2, 5):
                load_gain(k)
            for i, g in enumerate((gqa_q_norm, gqa_k_norm)):
                pool.dma_start(qk_gain[:, i, :], g.to_broadcast([P, HD])).then_inc(qk_gain_in, 16)
            for k in range(5, 8):
                load_gain(k)
            pool.dma_start(wr[:], moe_w_router[0].rearrange("(b p) e -> p b e", p=P)).then_inc(wr_in, 16)

        @block.scalar
        def _(act):
            split_at = [0]

            def split_until(end, job=None):
                for n in range(split_at[0], end):
                    base = 0 if job is None else job
                    act.wait_ge(landed[n % RAW], (base * (FFN_PIECES // RAW) + n // RAW + 1) * 16)
                    if n >= SPLIT:
                        act.wait_ge(piece_used, base * FFN_PIECES + n - SPLIT + 1)
                    act.activation(w_hi[:, n % SPLIT], raw[:, n % RAW], ACT.Copy).then_inc(hi_ready, 1)
                split_at[0] = end

            def root(k, t):
                act.wait_ge(meansq_ready, ROOTS[k, t])
                act.activation(std[:, t:t + 1], meansq[:, t:t + 1], ACT.Sqrt).then_inc(std_ready, 1)

            def free_junk(k, t, j):
                if SUMS[k, t, j] > 1:
                    act.wait_ge(sumsq_ready, SUMS[k, t, j] - 1)

            def square_h(k, t):
                free_junk(k, t, 0)
                if k == 0:
                    act.wait_ge(x_in[t], 16)
                else:
                    act.wait_ge(h_ready, T * (k // 2) - T + t + 1)
                act.activation(junk[:], h[:, t, :], ACT.Square, accum_out=sumsq[:, t, 0:1]).then_inc(sumsq_ready, 1)

            def square_product(k, t, j):
                free_junk(k, t, j)
                sig, count = product_ready(k, t, j)
                act.wait_ge(sig, count)
                act.activation(junk[:, 0:COLS], ps[:, PRODUCTS[k][1] + 2 * t + j, :], ACT.Square,
                               accum_out=sumsq[:, t, j:j + 1]).then_inc(sumsq_ready, 1)

            def keep_turned(k, t):
                act.wait_ge(nrm_turned, T * (k // 2) + t + 1)
                bank = TURN_BANK[k] + 2 * t
                act.activation(act_hi[:, :, t * P:(t + 1) * P],
                               ps[:, bank:bank + 2, :].rearrange("p b (c n) -> p (b c) n", c=4), ACT.Copy
                               ).then_inc(act_hi_ready, 1)

            def norms(k):
                after = PRODUCTS[k][2]
                act.preload_act_table(ACT.Sqrt)
                square_product(k, 0, 0)
                if k != 3:
                    square_product(k, 1, 0)
                    split_until(after + 1)
                square_product(k, 0, 1)
                root(k, 0)
                square_h(k + 1, 0)
                root(k + 1, 0)
                if k == 3:
                    split_until(after + 1)
                    square_product(k, 1, 0)
                square_product(k, 1, 1)
                root(k, 1)
                if k != 5:
                    keep_turned(k + 1, 0)
                split_until(after + 2)
                square_h(k + 1, 1)
                root(k + 1, 1)
                split_until(after + SPLIT)
                if k != 5:
                    keep_turned(k + 1, 1)

            def attention(i):
                s = att[i]
                units = 2 * HEADS // 4
                for u in range(units + 3):
                    if u >= 3:
                        act.wait_ge(s["o_ready"], u - 2)
                        dst, src = outputs(i, u - 3, act_hi)
                        act.activation(dst, src, ACT.Copy).then_inc(s["o_hi_ready"], 1)
                    if u < units:
                        act.wait_ge(s["max_ready"], u + 1)
                        if i == 1 and u >= 2:
                            act.wait_ge(s["probs_turned"], u - 1)
                        for q in range(4):
                            src = sc[:, u % 2, q, :] if i == 0 else ps[:, 2 * (u % 2) + q // 2,
                                                                      (q % 2) * SEQ:(q % 2 + 1) * SEQ]
                            last = act.activation(sc[:, u % 2, q, :], src, ACT.Exp, bias=nmax[:, u % 2, q:q + 1],
                                                  accum_out=psums[:, u % 2, q:q + 1])
                        last.then_inc(s["exp_ready"], 1)
                    if 1 <= u <= units:
                        act.wait_ge(s["probs_turned"], u)
                        if u >= 3:
                            act.wait_ge(s["o_ready"], u - 2)
                        act.activation(pT[:, (u - 1) % 2].rearrange("p a n -> p (a n)"),
                                       ps[:, 4:6, :].rearrange("p b n -> p (b n)"), ACT.Copy
                                       ).then_inc(s["pT_ready"], 1)

            for t in range(T):
                square_h(0, t)
                root(0, t)
            split_until(SPLIT)
            for t in range(T):
                keep_turned(0, t)
            for j in range(6):
                split_until(min(Q0 + 2 * j + 2 + 2, O0))
                act.wait_ge(piece_used, Q0 + 2 * j + 2)
                b = 4 * (j % 2)
                if j < 4:
                    chunks = slice(4 * (j % 2), 4 * (j % 2) + 4)
                    if j < 2:
                        act.activation(qT[:, chunks, :].rearrange("p b (r c) -> p b r c", c=GRID_W),
                                       rows_of(ps[:, b:b + 4, 0:SEQ]), ACT.Copy, scale=HD ** -0.5
                                       ).then_inc(qkv_kept[0], 1)
                    else:
                        act.activation(kT[:, chunks, :], ps[:, b:b + 4, 0:SEQ], ACT.Copy).then_inc(qkv_kept[0], 1)
                else:
                    act.activation(v0[:, :, (j - 4) * COLS:(j - 3) * COLS], ps[:, b:b + 2, :], ACT.Copy
                                   ).then_inc(qkv_kept[0], 1)
            act.preload_act_table(ACT.Exp)
            split_until(O0 + SPLIT)
            attention(0)
            split_until(F0)
            norms(1)
            act.preload_act_table(ACT.Silu)
            for s in range(STEPS):
                last = first_piece(s) + 3
                split_until(F0 + last + 3)
                act.wait_ge(piece_used, F0 + last + 1)
                act.activation(sil[:], ps[:, 0:4:2, :], ACT.Silu).then_inc(f0["silu"], 1)
                if s > 0:
                    split_until(F0 + min(last + 4, FFN_PIECES))
                act.wait_ge(f0["turned"], s + 1)
                act.activation(hT_hi[:, s % 2], ps[:, 0:4:2, :], ACT.Copy).then_inc(f0["hT_hi"], 1)
            split_until(Q1)
            norms(3)
            for j in range(3):
                heads = KV_HEADS if j == 0 else 8
                split_until(min(Q1 + 2 * j + 4, O1 + 2))
                act.wait_ge(piece_used, Q1 + 2 * j + 2)
                act.activation(rot_b[:, :, 0:heads * HD], ps[:, 2 * j:2 * j + 2, 0:heads * HD], ACT.Square
                               ).then_inc(heads_squared, 1)
                c0 = qkv1_columns[j]
                act.activation(qkv[:, :, c0:c0 + COLS], ps[:, 2 * j:2 * j + 2, :], ACT.Copy).then_inc(qkv_kept[1], 1)
                act.wait_ge(heads_ms, j + 1)
                act.activation(head_std[:, j, :, 0:heads], head_ms[:, j, :, 0:heads], ACT.Sqrt).then_inc(heads_std, 1)
                act.wait_ge(heads_turned, j + 1)
                src = ps[:, 6:8, :].rearrange("p t (c n) -> p c t n", c=4)
                dst = kT[:, 0:KV_HEADS, :] if j == 0 else qT[:, 4 * (j - 1):4 * j, :]
                act.activation(dst.rearrange("p c (t n) -> p c t n", t=T), src, ACT.Copy).then_inc(heads_kept, 1)
            act.preload_act_table(ACT.Exp)
            split_until(O1 + SPLIT)
            attention(1)
            split_until(J0)
            norms(5)
            act.preload_act_table(ACT.Exp)
            for t in range(T):
                act.wait_ge(nrm_turned, T * 3 + t + 1)
                act.activation(fT[:, :, t * P:(t + 1) * P],
                               ps[:, 4 + 2 * t:6 + 2 * t, :].rearrange("p b (c n) -> p (b c) n", c=4), ACT.Copy
                               ).then_inc(fT_ready, 1)
            for t in range(T):
                act.activation(tok_hi[:, t, :], nrm[:, t, :], ACT.Copy).then_inc(tok_hi_ready, 1)
            act.wait_ge(logits_kept, 1)
            for t in range(T):
                act.activation(gate[:, t, :], logit[:, t, :], ACT.Exp, bias=r1[:, t:t + 1]).then_inc(logits_exp, 1)
            act.preload_act_table(ACT.Silu)

            def keep_gathered(j):
                act.wait_ge(gathered, j + 1)
                act.activation(act_hi[:, :, 0:P], ps[:, 6:8, :].rearrange("p b (c n) -> p (b c) n", c=4), ACT.Copy
                               ).then_inc(x_hi_ready, 1)

            def expert_job(j):
                split_at[0] = max(J0, J0 + SPLIT if isinstance(j, int) else J0)
                split_until(J0 + SPLIT, j)
                act.wait_ge(pick_turned, j + 1)
                if not isinstance(j, int):
                    act.wait_ge(scattered, j)
                act.activation(pick_gT[:], ps[:, 1, 0:T * P].rearrange("p (t n) -> p t n", t=T), ACT.Copy
                               ).then_inc(pickT_ready, 1)
                for s in range(STEPS):
                    split_until(J0 + 6 * s + (4 if s else 6), j)
                    act.wait_ge(piece_used, j * FFN_PIECES + (J0 + first_piece(s) + 4))
                    act.activation(sil[:, 0, :], ps[:, 2 * (s % 2), :], ACT.Silu).then_inc(fj["silu"], 1)
                    split_until(J0 + min(6 * s + 8, FFN_PIECES), j)
                    act.wait_ge(fj["turned"], j * STEPS + s + 1)
                    act.activation(hT_hi[:, 0, 0, :], ps[:, 2 * (s % 2), :], ACT.Copy).then_inc(fj["hT_hi"], 1)
                keep_gathered(j + 1)
                act.wait_ge(piece_used, j * FFN_PIECES + (J0 + FFN_PIECES))
                act.activation(y_sb[:], ps[:, 4:6, :].rearrange("p b n -> p (b n)"), ACT.Copy).then_inc(y_kept, 1)

            keep_gathered(0)
            expert_job(0)
            with act.Fori(1, E) as j:
                expert_job(j)
            act.wait_ge(over_ready, 1)
            n_over = act.value_load(over[0:1, 0:1], min_val=0, max_val=MAX_OVER)
            with act.If(n_over > 0):
                with act.Fori(0, n_over) as i:
                    expert_job(i + E)
            act.preload_act_table(ACT.Sqrt)
            for t in range(T):
                free_junk(7, t, 0)
                act.wait_ge(y_added, (n_over + E) * T + t + 1)
                act.activation(junk[:], nrm[:, t, :], ACT.Square, accum_out=sumsq[:, t, 0:1]).then_inc(sumsq_ready, 1)
                root(7, t)

        @block.vector
        def _(dve):
            split_at = [0]
            links = [0]

            def link(ins):
                links[0] += 1
                ins.then_inc(dve_chain, 1)
                dve.wait_ge(dve_chain, links[0])

            def split_until(end, job=None):
                for n in range(split_at[0], end):
                    base = 0 if job is None else job
                    dve.wait_ge(hi_ready, base * FFN_PIECES + n + 1)
                    dve.tensor_tensor(w_lo[:, n % SPLIT], raw[:, n % RAW], w_hi[:, n % SPLIT].bitcast(F32),
                                      ALU.subtract).then_inc(lo_ready, 1)
                split_at[0] = end

            def mean_square(k, t, first_half=None):
                dve.wait_ge(sumsq_ready, SUMS[k, t, 0 if first_half is None else 1])
                if first_half is None:
                    ins = dve.tensor_scalar(meansq[:, t:t + 1], sumsq[:, t, 0:1], 1.0 / D, EPS, ALU.mult, ALU.add)
                else:
                    ins = dve.tensor_scalar(meansq[:, t:t + 1], sumsq[:, t, 1:2], 1.0 / D, first_half,
                                            ALU.mult, ALU.add)
                ins.then_inc(meansq_ready, 1)

            def inverse(k, t):
                dve.wait_ge(std_ready, ROOTS[k, t])
                link(dve.reciprocal(rstd[:, t:t + 1], std[:, t:t + 1]))

            def normalise(k, t):
                inverse(k, t)
                dve.scalar_tensor_tensor(nrm[:, t, :], h[:, t, :], rstd[:, t:t + 1], gain[:, 0, :],
                                         ALU.mult, ALU.mult).then_inc(nrm_ready, 1)

            def keep_turned(k, t):
                dve.wait_ge(act_hi_ready, T * (k // 2) + t + 1)
                bank = TURN_BANK[k] + 2 * t
                tok = slice(t * P, (t + 1) * P)
                dve.tensor_tensor(act_lo[:, :, tok], ps[:, bank:bank + 2, :].rearrange("p b (c n) -> p (b c) n", c=4),
                                  act_hi[:, :, tok].bitcast(F32), ALU.subtract).then_inc(act_ready, 1)

            def norms(k):
                n, bank, after = PRODUCTS[k]

                def scale(t, j):
                    dve.wait_ge(sumsq_ready, SUMS[k, t, j])
                    cols = slice(j * COLS, (j + 1) * COLS)
                    dve.tensor_tensor(nrm[:, t, cols], ps[:, bank + 2 * t + j, :], gain[:, 1, cols], ALU.mult
                                      ).then_inc(scaled_ready, 1)
                    if j == 0:
                        link(dve.tensor_scalar(part[:, t:t + 1], sumsq[:, t, 0:1], 1.0 / D, EPS, ALU.mult, ALU.add))

                def add(t):
                    mean_square(k, t, part[:, t:t + 1])
                    scale(t, 1)
                    inverse(k, t)
                    done = 2 * T if t == 1 else 2 if k == 3 else 3
                    dve.wait_ge(scaled_ready, 2 * T * (k // 2) + done)
                    dve.scalar_tensor_tensor(h[:, t, :], nrm[:, t, :], rstd[:, t:t + 1], h[:, t, :],
                                             ALU.mult, ALU.add).then_inc(h_ready, 1)
                    dve.wait_ge(h_ready, T * (k // 2) + t + 1)

                dve.wait_ge(gain_in[1], 16 * (k // 2 + 1))
                dve.wait_ge(gain_in[0], 16 * ((k + 1) // 2 + 1))
                scale(0, 0)
                if k != 3:
                    scale(1, 0)
                    split_until(after + 1)
                add(0)
                mean_square(k + 1, 0)
                normalise(k + 1, 0)
                if k == 3:
                    split_until(after + 1)
                    scale(1, 0)
                add(1)
                if k != 5:
                    keep_turned(k + 1, 0)
                split_until(after + 2)
                mean_square(k + 1, 1)
                normalise(k + 1, 1)
                dve.wait_ge(nrm_ready, T * ((k + 1) // 2 + 1))
                dve.sem_inc(gain_used, 2)
                split_until(after + SPLIT)
                if k != 5:
                    keep_turned(k + 1, 1)

            def attention(i):
                s = att[i]
                units = 2 * HEADS // 4
                for u in range(units + 3):
                    if u < units:
                        a, t = u // 2, u % 2
                        dve.wait_ge(s["scores_ready"], u + 1)
                        banks = ps[:, 2 * (u % 2):2 * (u % 2) + 2, :]
                        if i == 0:
                            if u >= 2:
                                dve.wait_ge(s["probs_turned"], u - 1)
                            for q in range(4):
                                par, b = q // 2, q % 2
                                link_max = dve.tensor_tensor_reduce(
                                    sc[:, u % 2, q, :], banks[:, par, b * SEQ:(b + 1) * SEQ],
                                    bias[:, 4 * a + par + 2 * b, 2 - 2 * t:6 - 2 * t, :].rearrange("p i n -> p (i n)"),
                                    1.0, -3e38, ALU.add, ALU.max, pmax[:, u % 2, q:q + 1])
                            link_max.then_inc(s["biased"], 1)
                            dve.wait_ge(s["biased"], u + 1)
                            dve.tensor_scalar(nmax[:, u % 2, :], pmax[:, u % 2, :], -1.0, None, ALU.mult
                                              ).then_inc(s["max_ready"], 1)
                        else:
                            dve.tensor_reduce(nmax[:, u % 2, :], banks.rearrange("p b (c n) -> p (b c) n", c=2),
                                              AX.X, ALU.max, negate=True).then_inc(s["max_ready"], 1)
                    if 1 <= u <= units:
                        half = (u - 1) % 2
                        dve.wait_ge(s["exp_ready"], u)
                        link(dve.reciprocal(rsums[:, half, :], psums[:, half, :]))
                        for q in range(4):
                            last = dve.tensor_scalar(sc[:, half, q, :], sc[:, half, q, :], rsums[:, half, q:q + 1],
                                                     None, ALU.mult)
                        last.then_inc(s["probs_ready"], 1)
                    if u >= 3:
                        dve.wait_ge(s["o_hi_ready"], u - 2)
                        lo, src = outputs(i, u - 3, act_lo)
                        hi, _ = outputs(i, u - 3, act_hi.bitcast(F32))
                        dve.tensor_tensor(lo, src, hi, ALU.subtract).then_inc(s["o_split"], 1)

            def head_tables():
                dve.wait_ge(qk_gain_in, 32)
                for g, scale in enumerate((HD ** -0.5, 1.0)):
                    for t in range(T):
                        cos = cst[:, C_COS + t * HD:C_COS + (t + 1) * HD]
                        sin = cst[:, C_SIN + t * HD:C_SIN + (t + 1) * HD].rearrange("p (a b f) -> p a b f", a=2, b=2)
                        swapped = qk_sin[:, g, t, :].rearrange("p (a b f) -> p a b f", a=2, b=2)
                        other = qk_gain[:, g, :].rearrange("p (a b f) -> p a b f", a=2, b=2)
                        link(dve.scalar_tensor_tensor(qk_cos[:, g, t, :], cos, scale, qk_gain[:, g, :],
                                                      ALU.mult, ALU.mult))
                        for b in range(2):
                            link(dve.scalar_tensor_tensor(swapped[:, :, b, :], sin[:, :, b, :], scale,
                                                          other[:, :, 1 - b, :], ALU.mult, ALU.mult))

            def rotate_heads(j):
                n = KV_HEADS if j == 0 else 8
                g = 1 if j == 0 else 0
                c0 = qkv1_columns[j]
                own = qkv[:, :, c0:c0 + n * HD].rearrange("p t (n d) -> p t n d", d=HD)
                ra = rot_a[:, :, 0:n * HD].rearrange("p t (n d) -> p t n d", d=HD)
                rb = rot_b[:, :, 0:n * HD].rearrange("p t (n d) -> p t n d", d=HD)
                dve.wait_ge(heads_squared, j + 1)
                link(dve.tensor_reduce(head_ss[:, j, :, 0:n], rb, AX.X, ALU.add))
                dve.tensor_scalar(head_ms[:, j, :, 0:n], head_ss[:, j, :, 0:n], 1.0 / HD, EPS, ALU.mult, ALU.add
                                  ).then_inc(heads_ms, 1)
                dve.wait_ge(qkv_kept[1], j + 1)
                dve.tensor_tensor(ra, own, qk_cos[:, g].unsqueeze(2).to_broadcast([P, T, n, HD]), ALU.mult)
                for t in range(T):
                    x = own[:, t].rearrange("p n (a b f) -> p n a b f", a=2, b=2)
                    o = rb[:, t].rearrange("p n (a b f) -> p n a b f", a=2, b=2)
                    sin = qk_sin[:, g, t, :].rearrange("p (a b f) -> p a b f", a=2, b=2)
                    for b in range(2):
                        last = dve.tensor_tensor(o[:, :, :, b, :], x[:, :, :, 1 - b, :],
                                                 sin[:, :, b, :].unsqueeze(1).to_broadcast([P, n, 2, HD // 4]),
                                                 ALU.mult)
                link(last)
                link(dve.tensor_tensor(ra, ra, rb, ALU.add))
                dve.wait_ge(heads_std, j + 1)
                link(dve.reciprocal(head_rs[:, j, :, 0:n], head_std[:, j, :, 0:n]))
                rs = head_rs[:, j, :, 0:n].unsqueeze(3).to_broadcast([P, T, n, HD])
                if j == 0:
                    for copy in range(2):
                        last = dve.tensor_tensor(kdup[:, :, :, copy, :], ra, rs, ALU.mult)
                else:
                    last = dve.tensor_tensor(own, ra, rs, ALU.mult)
                last.then_inc(heads_ready, 1)

            dve.wait_ge(gain_in[0], 16)
            for t in range(T):
                mean_square(0, t)
                normalise(0, t)
            dve.wait_ge(nrm_ready, T)
            dve.sem_inc(gain_used, 1)
            split_until(SPLIT)
            for t in range(T):
                keep_turned(0, t)
            split_until(O0 + SPLIT)
            dve.wait_ge(bias_masked, 4)
            attention(0)
            split_until(F0)
            norms(1)
            for s in range(STEPS):
                last = first_piece(s) + 3
                split_until(F0 + last + 3)
                dve.wait_ge(f0["silu"], s + 1)
                dve.tensor_tensor(hid[:], sil[:], ps[:, 1:4:2, :], ALU.mult).then_inc(f0["hid"], 1)
                if s > 0:
                    split_until(F0 + min(last + 4, FFN_PIECES))
                dve.wait_ge(f0["hT_hi"], s + 1)
                dve.tensor_tensor(hT_lo[:, s % 2], ps[:, 0:4:2, :], hT_hi[:, s % 2].bitcast(F32), ALU.subtract
                                  ).then_inc(f0["hT"], 1)
            split_until(Q1)
            norms(3)
            head_tables()
            for j in range(3):
                split_until(min(Q1 + 2 * j + 4, O1 + 2))
                rotate_heads(j)
            split_until(O1 + SPLIT)
            attention(1)
            split_until(J0)
            norms(5)

            def over_pairs(ap):
                return (ap.unsqueeze(2).to_broadcast([P, T, E, E]), ap.unsqueeze(3).to_broadcast([P, T, E, E]))

            dve.wait_ge(logits_ready, 1)
            link(dve.tensor_copy(logit[:], ps[:, 0, 0:T * E].rearrange("p (t e) -> p t e", t=T)))
            dve.tensor_reduce(r1[:, 0:T], logit[:], AX.X, ALU.max, negate=True).then_inc(logits_kept, 1)
            tri = cst[:, C_TRI:C_TRI + E * E]
            lj = logit[:].unsqueeze(2).to_broadcast([P, T, E, E])
            le = logit[:].unsqueeze(3).to_broadcast([P, T, E, E])
            dve.tensor_tensor(pair[:], lj, le, ALU.is_gt)
            link(dve.tensor_tensor(pair2[:], lj, le, ALU.is_equal))
            link(dve.tensor_tensor(pair2[:].rearrange("p t e j -> p t (e j)"), pair2[:].rearrange("p t e j -> p t (e j)"),
                                   tri.unsqueeze(1).to_broadcast([P, T, E * E]), ALU.mult))
            link(dve.tensor_tensor(pair[:], pair[:], pair2[:], ALU.add))
            link(dve.tensor_reduce(prod8[:], pair[:], AX.X, ALU.add))
            dve.tensor_scalar(chosen[:], prod8[:], float(TOP_K), None, ALU.is_lt).then_inc(chosen_ready, 1)
            dve.wait_ge(chosen_ready, 1)
            dve.wait_ge(logits_exp, T)
            link(dve.tensor_tensor(gate[:], gate[:], chosen[:], ALU.mult))
            link(dve.tensor_reduce(r1[:, 2:2 + T], gate[:], AX.X, ALU.add))
            link(dve.reciprocal(r1[:, 4:4 + T], r1[:, 2:2 + T]))
            for t in range(T):
                link(dve.tensor_scalar(job_gate[:, t, 0:E], gate[:, t, :], r1[:, 4 + t:5 + t], None, ALU.mult))
            dve.wait_ge(pos_ready, 1)
            link(dve.scalar_tensor_tensor(pos[:], ps[:, 1, 0:T * E].rearrange("p (t e) -> p t e", t=T), 1.0,
                                          chosen[:], ALU.add, ALU.mult))
            full = r8[:, 0, :]
            link(dve.tensor_scalar(full, ps[:, 1, T * E:(T + 1) * E], float(P), None, ALU.is_gt))
            link(dve.tensor_scalar(job_pos[:, :, 0:E], pos[:], -1.0, None, ALU.add))

            def overflow_jobs():
                before, mine = r8[:, 1, :], r8[:, 2, :]
                link(dve.tensor_tensor(pair[:, 0], full.unsqueeze(1).to_broadcast([P, E, E]),
                                       tri.rearrange("p (e j) -> p e j", e=E), ALU.mult))
                link(dve.tensor_reduce(before, pair[:, 0], AX.X, ALU.add))
                link(dve.tensor_reduce(over_f[:, 0:1], full, AX.X, ALU.add))
                far = 1000.0
                link(dve.tensor_scalar(pos[:], pos[:], far - P - 1, None, ALU.add))
                link(dve.memset(job_pos[:, :, E + MAX_OVER:JOB_COLS], -1.0))
                link(dve.memset(job_gate[:, :, E + MAX_OVER:JOB_COLS], 0.0))
                for i in range(MAX_OVER):
                    link(dve.tensor_scalar(mine, before, float(i), None, ALU.is_equal))
                    link(dve.tensor_tensor(mine, mine, full, ALU.mult))
                    link(dve.tensor_tensor(r8[:, 3, :], mine, cst[:, C_EXP:C_EXP + E], ALU.mult))
                    link(dve.tensor_reduce(over_f[:, 1 + i:2 + i], r8[:, 3, :], AX.X, ALU.add))
                    for src, dst in ((pos[:], job_pos), (job_gate[:, :, 0:E], job_gate)):
                        link(dve.tensor_tensor(prod8[:], src, mine.unsqueeze(1).to_broadcast([P, T, E]), ALU.mult))
                        link(dve.tensor_reduce(dst[:, :, E + i:E + i + 1], prod8[:], AX.X, ALU.add))
                link(dve.tensor_scalar(job_pos[:, :, E:E + MAX_OVER], job_pos[:, :, E:E + MAX_OVER], -far, None,
                                       ALU.add))
                dve.tensor_copy(over[:], over_f[:]).then_inc(over_ready, 1)

            def build_pick(j):
                if not isinstance(j, int) or j > 0:
                    dve.wait_ge(pick_turned, j)
                column = bass.ds(j, 1)
                dve.tensor_copy(cur[:, 0, :].unsqueeze(2), job_pos[:, :, column]).then_inc(cur_ready, 1)
                dve.tensor_copy(cur[:, 1, :].unsqueeze(2), job_gate[:, :, column]).then_inc(cur_ready, 1)
                dve.wait_ge(cur_ready, 2 * j + 2)
                iota = cst[:, C_IOTA:C_IOTA + P]
                for t in range(T):
                    dve.tensor_scalar(pick[:, t, :], iota, cur[:, 0, t:t + 1], None, ALU.is_equal
                                      ).then_inc(pick_ready, 1)
                    dve.tensor_scalar(pick_g[:, t, :], iota, cur[:, 0, t:t + 1], cur[:, 1, t:t + 1],
                                      ALU.is_equal, ALU.mult).then_inc(pick_ready, 1)

            def keep_gathered(j):
                dve.wait_ge(x_hi_ready, j + 1)
                dve.tensor_tensor(act_lo[:, :, 0:P], ps[:, 6:8, :].rearrange("p b (c n) -> p (b c) n", c=4),
                                  act_hi[:, :, 0:P].bitcast(F32), ALU.subtract).then_inc(x_ready, 1)

            def add_outputs(j):
                dve.wait_ge(scattered, j + 1)
                for t, b in enumerate((4, 2)):
                    dve.tensor_tensor(nrm[:, t, :], nrm[:, t, :],
                                      ps[:, b:b + 2, :].rearrange("p b n -> p (b n)"), ALU.add).then_inc(y_added, 1)

            def expert_job(j):
                first = isinstance(j, int)
                split_at[0] = J0 + SPLIT if first else J0
                split_until(J0 + SPLIT, j)
                if not first:
                    dve.wait_ge(y_added, T * j)
                    add_outputs(j - 1)
                for s in range(STEPS):
                    split_until(J0 + 6 * s + (4 if s else 6), j)
                    dve.wait_ge(fj["silu"], j * STEPS + s + 1)
                    dve.tensor_tensor(hid[:, 0, :], sil[:, 0, :], ps[:, 2 * (s % 2) + 1, :], ALU.mult
                                      ).then_inc(fj["hid"], 1)
                    if s == STEPS - 1:
                        build_pick(j + 1)
                    split_until(J0 + min(6 * s + 8, FFN_PIECES), j)
                    dve.wait_ge(fj["hT_hi"], j * STEPS + s + 1)
                    dve.tensor_tensor(hT_lo[:, 0, 0, :], ps[:, 2 * (s % 2), :], hT_hi[:, 0, 0, :].bitcast(F32),
                                      ALU.subtract).then_inc(fj["hT"], 1)
                keep_gathered(j + 1)

            build_pick(0)
            for t in range(T):
                dve.wait_ge(tok_hi_ready, t + 1)
                dve.tensor_tensor(tok_lo[:, t, :], nrm[:, t, :], tok_hi[:, t, :].bitcast(F32), ALU.subtract
                                  ).then_inc(tok_ready, 1)
            dve.wait_ge(nrm_turned, 4 * T)
            dve.wait_ge(tok_ready, T)
            for t in range(T):
                dve.memset(nrm[:, t, :], 0.0).then_inc(y_added, 1)
            keep_gathered(0)
            overflow_jobs()
            expert_job(0)
            with dve.Fori(1, E) as j:
                expert_job(j)
            dve.wait_ge(over_ready, 1)
            n_over = dve.value_load(over[0:1, 0:1], min_val=0, max_val=MAX_OVER)
            with dve.If(n_over > 0):
                with dve.Fori(0, n_over) as i:
                    expert_job(i + E)
            dve.wait_ge(y_added, (n_over + E) * T)
            add_outputs(n_over + (E - 1))
            dve.wait_ge(gain_in[1], 16 * 4)
            for t in range(T):
                mean_square(7, t)
                inverse(7, t)
                link(dve.scalar_tensor_tensor(nrm[:, t, :], nrm[:, t, :], rstd[:, t:t + 1], gain[:, 1, :],
                                              ALU.mult, ALU.mult))
                dve.tensor_tensor(h[:, t, :], h[:, t, :], nrm[:, t, :], ALU.add).then_inc(h_ready, 1)

        @block.tensor
        def _(pe):
            def product(out, hi, lo, slot, b, start, stop):
                wh, wl = w_hi[:, slot, b, :], w_lo[:, slot, b, :]
                pe.matmul(out, hi, wh, start=start, stop=False)
                pe.matmul(out, hi, wl, start=False, stop=False)
                return pe.matmul(out, lo, wh, start=False, stop=stop)

            def take(n, job=None):
                pe.wait_ge(lo_ready, (0 if job is None else job * FFN_PIECES) + n + 1)

            def turn_norm(k, t):
                if k == 0 and t == 0:
                    pe.wait_ge(cst_in, 16)
                pe.wait_ge(nrm_ready, T * (k // 2) + t + 1)
                for c in range(KC):
                    ins = pe.transpose(ps[:, TURN_BANK[k] + 2 * t + c // 4, (c % 4) * P:(c % 4 + 1) * P],
                                       nrm[:, t, c * P:(c + 1) * P], ident)
                ins.then_inc(nrm_turned, 1)

            def token_blocks(n, half, t, bank):
                for b in range(PK):
                    c = PK * half + b
                    tok = slice(t * P, (t + 1) * P)
                    last = product(ps[:, bank, :], act_hi[:, c, tok], act_lo[:, c, tok], n % SPLIT, b,
                                   c == 0, c == KC - 1)
                return last

            def two_pieces(n, banks):
                for half in range(2):
                    take(n + half)
                    for t in range(T):
                        last = token_blocks(n + half, half, t, banks(t))
                    last.then_inc(piece_used, 1)

            def two_pieces_turning(n, banks, k):
                turn_norm(k, 0)
                pe.wait_ge(act_ready, T * (k // 2) + 1)
                for t in range(T):
                    if t == 1:
                        turn_norm(k, 1)
                        pe.wait_ge(act_ready, T * (k // 2) + 2)
                    for half in range(2):
                        if t == 0:
                            take(n + half)
                        last = token_blocks(n + half, half, t, banks(t))
                        if t == 1:
                            last.then_inc(piece_used, 1)

            def output_product(n):
                two_pieces(n, lambda t: 2 * t)
                for t in range(T):
                    for half in range(2):
                        if t == 0:
                            take(n + 2 + half)
                        last = token_blocks(n + 2 + half, half, t, 2 * t + 1)
                        if t == 1:
                            last.then_inc(piece_used, 1)
                    if t == 0:
                        last.then_inc(tile0_done, 1)

            def attention(i, kv_chunk, value):
                s = att[i]
                units = 2 * HEADS // 4

                def scores(u):
                    a, t = u // 2, u % 2
                    if u >= 2:
                        pe.wait_ge(s["biased"] if i == 0 else s["exp_ready"], u - 1)
                    for b in range(2):
                        for par in range(2):
                            head = 4 * a + 2 * b + par
                            rows = slice(par * HD, (par + 1) * HD)
                            last = pe.matmul(ps[:, 2 * (u % 2) + par, b * SEQ:(b + 1) * SEQ],
                                             qT[rows, head // 2, t * P:(t + 1) * P],
                                             kT[rows, kv_chunk(head), :], start=True, stop=True)
                    last.then_inc(s["scores_ready"], 1)

                scores(0)
                for u in range(units + 2):
                    if u + 1 < units:
                        scores(u + 1)
                    if 1 <= u <= units:
                        pe.wait_ge(s["probs_ready"], u)
                        if u >= 2:
                            pe.wait_ge(s["pT_ready"], u - 1)
                        for q in range(4):
                            for c in range(2):
                                m = 2 * (q % 2) + c
                                last = pe.transpose(ps[:, 4 + q // 2, m * P:(m + 1) * P],
                                                    sc[:, (u - 1) % 2, q, c * P:(c + 1) * P], ident)
                        last.then_inc(s["probs_turned"], 1)
                    if u >= 2:
                        w = u - 2
                        pe.wait_ge(s["pT_ready"], w + 1)
                        if w >= 2:
                            pe.wait_ge(s["o_split"], w - 1)
                        for q in range(4):
                            par, b = q // 2, q % 2
                            head = 4 * (w // 2) + 2 * b + par
                            for c in range(2):
                                last = pe.matmul(ps[par * HD:(par + 1) * HD, 6 + w % 2, b * P:(b + 1) * P],
                                                 value(c, head), pT[:, w % 2, 2 * q + c, :],
                                                 start=(c == 0), stop=(c == 1))
                        last.then_inc(s["o_ready"], 1)

            def down_blocks(n, s, half, buf, t, bank):
                for b in range(PK):
                    last = product(ps[:, bank + half, :], hT_hi[:, buf, t, b * P:(b + 1) * P],
                                   hT_lo[:, buf, t, b * P:(b + 1) * P], n % SPLIT, b,
                                   s == 0 and b == 0, s == STEPS - 1 and b == PK - 1)
                return last

            for t in range(T):
                turn_norm(0, t)
            pe.wait_ge(act_ready, T)
            for j in range(4):
                if j >= 2:
                    pe.wait_ge(qkv_kept[0], j - 1)
                for half in range(2):
                    n = Q0 + 2 * j + half
                    take(n)
                    for b in range(PK):
                        c = PK * half + b
                        for m in range(4):
                            o = ps[:, 4 * (j % 2) + m, 0:SEQ]
                            wh = w_hi[:, n % SPLIT, b, m * P:(m + 1) * P]
                            wl = w_lo[:, n % SPLIT, b, m * P:(m + 1) * P]
                            pe.matmul(o, wh, act_hi[:, c, :], start=(c == 0), stop=False)
                            pe.matmul(o, wh, act_lo[:, c, :], start=False, stop=False)
                            last = pe.matmul(o, wl, act_hi[:, c, :], start=False, stop=(c == KC - 1))
                    last.then_inc(piece_used, 1)
            for j in range(4, 6):
                pe.wait_ge(qkv_kept[0], j - 1)
                two_pieces(Q0 + 2 * j, lambda t: 4 * (j % 2) + t)
            pe.wait_ge(qkv_kept[0], 6)
            attention(0, lambda head: head // 2, lambda c, head: v0[:, c, head * HD:(head + 1) * HD])
            pe.wait_ge(att[0]["o_split"], 8)
            output_product(O0)

            for s in range(STEPS):
                n = F0 + first_piece(s)
                if s == 0:
                    two_pieces_turning(n, lambda t: 2 * t, 2)
                else:
                    pe.wait_ge(f0["hT"], s)
                    two_pieces(n, lambda t: 2 * t)
                two_pieces(n + 2, lambda t: 2 * t + 1)
                if s >= 1:
                    take(n + 4)
                    for t in range(T):
                        last = down_blocks(n + 4, s - 1, 0, (s - 1) % 2, t, 4 + 2 * t)
                    last.then_inc(piece_used, 1)
                pe.wait_ge(f0["hid"], s + 1)
                for t in range(T):
                    for b in range(PK):
                        last = pe.transpose(ps[:, 2 * t, b * P:(b + 1) * P], hid[:, t, b * P:(b + 1) * P], ident)
                last.then_inc(f0["turned"], 1)
                if s >= 1:
                    take(n + 5)
                    for t in range(T):
                        last = down_blocks(n + 5, s - 1, 1, (s - 1) % 2, t, 4 + 2 * t)
                    last.then_inc(piece_used, 1)
            pe.wait_ge(f0["hT"], STEPS)
            for t in range(T):
                for half in range(2):
                    n = Q1 - 2 + half
                    if t == 0:
                        take(n)
                    last = down_blocks(n, STEPS - 1, half, (STEPS - 1) % 2, t, 4 + 2 * t)
                    last.then_inc(tile0_done if t == 0 else piece_used, 1)

            def turn_heads(j):
                pe.wait_ge(heads_ready, j + 1)
                if j > 0:
                    pe.wait_ge(heads_kept, j)
                for t in range(T):
                    for c in range(4):
                        if j == 0:
                            src = kdup[:, t, c].rearrange("p a d -> p (a d)")
                        else:
                            src = qkv[:, t, qkv1_columns[j] + c * P:qkv1_columns[j] + (c + 1) * P]
                        last = pe.transpose(ps[:, 6 + t, c * P:(c + 1) * P], src, ident)
                last.then_inc(heads_turned, 1)

            two_pieces_turning(Q1, lambda t: t, 4)
            two_pieces(Q1 + 2, lambda t: 2 + t)
            turn_heads(0)
            two_pieces(Q1 + 4, lambda t: 4 + t)
            turn_heads(1)
            turn_heads(2)
            pe.wait_ge(heads_kept, 3)
            v_at = NQ + NKV
            attention(1, lambda head: head // 4,
                      lambda c, head: qkv[:, c, v_at + (head // 4) * HD:v_at + (head // 4 + 1) * HD])
            pe.wait_ge(att[1]["o_split"], 8)
            output_product(O1)

            for t in range(T):
                turn_norm(6, t)
            pe.wait_ge(wr_in, 16)
            pe.wait_ge(fT_ready, T)
            for t in range(T):
                for c in range(KC):
                    last = pe.matmul(ps[:, 0, t * E:(t + 1) * E], fT[:, c, t * P:(t + 1) * P], wr[:, c, :],
                                     start=(c == 0), stop=(c == KC - 1))
            last.then_inc(logits_ready, 1)
            pe.wait_ge(chosen_ready, 1)
            before, ones = cst[:, C_BEFORE:C_BEFORE + P], cst[:, C_ONES:C_ONES + P]
            pe.matmul(ps[:, 1, 0:E], before, chosen[:, 0, :], start=True, stop=True)
            pe.matmul(ps[:, 1, E:2 * E], ones, chosen[:, 0, :], start=True, stop=False)
            pe.matmul(ps[:, 1, E:2 * E], before, chosen[:, 1, :], start=False, stop=True)
            pe.matmul(ps[:, 1, 2 * E:3 * E], ones, chosen[:, 0, :], start=True, stop=False)
            pe.matmul(ps[:, 1, 2 * E:3 * E], ones, chosen[:, 1, :], start=False, stop=True).then_inc(pos_ready, 1)

            def gather(j):
                pe.wait_ge(pick_ready, 4 * j + 4)
                for c in range(KC):
                    o = ps[:, 6 + c // 4, (c % 4) * P:(c % 4 + 1) * P]
                    for t in range(T):
                        pe.matmul(o, tok_hi[:, t, c * P:(c + 1) * P], pick[:, t, :], start=(t == 0), stop=False)
                        last = pe.matmul(o, tok_lo[:, t, c * P:(c + 1) * P], pick[:, t, :], start=False,
                                         stop=(t == T - 1))
                last.then_inc(gathered, 1)

            def turn_pick():
                for t in range(T):
                    last = pe.transpose(ps[:, 1, t * P:(t + 1) * P], pick_g[:, t, :], ident)
                last.then_inc(pick_turned, 1)

            def expert_job(j):
                pe.wait_ge(x_ready, j + 1)
                for s in range(STEPS):
                    n = J0 + first_piece(s)
                    q = 2 * (s % 2)
                    if s == 1:
                        pe.wait_ge(y_added, T * j + T)
                    for m in range(4):
                        if s == 0 and m == 2:
                            pe.wait_ge(pickT_ready, j + 1)
                        take(n + m, j)
                        for b in range(PK):
                            c = PK * (m % 2) + b
                            last = product(ps[:, q + m // 2, :], act_hi[:, c, 0:P], act_lo[:, c, 0:P],
                                           (n + m) % SPLIT, b, c == 0, c == KC - 1)
                        last.then_inc(piece_used, 1)
                        if m == 1 and s >= 1:
                            turn_hidden(j, s - 1)
                    if s >= 1:
                        pe.wait_ge(fj["hT"], j * STEPS + s)
                        for half in range(2):
                            take(n + 4 + half, j)
                            down_blocks(n + 4 + half, s - 1, half, 0, 0, 4).then_inc(piece_used, 1)
                turn_hidden(j, STEPS - 1)
                gather(j + 1)
                pe.wait_ge(fj["hT"], j * STEPS + STEPS)
                for half in range(2):
                    n = J0 + FFN_PIECES - 2 + half
                    take(n, j)
                    down_blocks(n, STEPS - 1, half, 0, 0, 4).then_inc(piece_used, 1)
                pe.wait_ge(y_kept, j + 1)
                for t, bank in enumerate((4, 2)):
                    for half in range(2):
                        last = pe.matmul(ps[:, bank + half, :], pick_gT[:, t, :],
                                         y_sb[:, half * COLS:(half + 1) * COLS], start=True, stop=True)
                last.then_inc(scattered, 1)
                turn_pick()

            def turn_hidden(j, s):
                pe.wait_ge(fj["hid"], j * STEPS + s + 1)
                for b in range(PK):
                    last = pe.transpose(ps[:, 2 * (s % 2), b * P:(b + 1) * P], hid[:, 0, b * P:(b + 1) * P], ident)
                last.then_inc(fj["turned"], 1)

            pe.wait_ge(tok_ready, T)
            gather(0)
            turn_pick()
            expert_job(0)
            with pe.Fori(1, E) as j:
                expert_job(j)
            pe.wait_ge(over_ready, 1)
            n_over = pe.value_load(over[0:1, 0:1], min_val=0, max_val=MAX_OVER)
            with pe.If(n_over > 0):
                with pe.Fori(0, n_over) as i:
                    expert_job(i + E)


_INS = ["x", "norm_g", "na_w_qkv", "na_rpb", "na_w_o", "gqa_w_qkv", "gqa_q_norm", "gqa_k_norm", "gqa_w_o",
        "ffn_w_gate", "ffn_w_up", "ffn_w_down", "moe_w_router", "moe_w_gate", "moe_w_up", "moe_w_down"]


def kernel(**inputs):
    import concourse.bacc as bacc
    from concourse.bass_utils import run_bass_kernel_spmd

    nc = bacc.Bacc("TRN2", target_bir_lowering=False, num_devices=1)
    arrays, args = {}, []
    for name in _INS:
        a = np.ascontiguousarray(inputs[name])
        arrays[f"in_{name}"] = a
        args.append(nc.dram_tensor(f"in_{name}", a.shape, mybir.dt.from_np(a.dtype), kind="ExternalInput").ap())
    arrays["in_consts"] = constants()
    args.append(nc.dram_tensor("in_consts", (P, C_ALL), F32, kind="ExternalInput").ap())
    args.append(nc.dram_tensor("out_0", (1, SEQ, D), F32, kind="ExternalOutput").ap())
    encoder_kernel(nc, *args)
    r = run_bass_kernel_spmd(nc, [arrays], core_ids=[0])
    return r.results[0]["out_0"]
```

```python
from contextlib import ExitStack

import numpy as np

import concourse.bass as bass
from concourse import mybir

F32 = mybir.dt.float32
F32R = mybir.dt.float32r
I32 = mybir.dt.int32
ACT = mybir.ActivationFunctionType
ALU = mybir.AluOpType
AX = mybir.AxisListType

P = 128
D = 1024
SEQ = 256
T = SEQ // P
KC = D // P
GRID_W = 64
ROWS = SEQ // GRID_W
HEADS = 16
HD = 64
KV_HEADS = 4
WIN_H, WIN_W = 8, 16
RPB_H, RPB_W = 2 * WIN_H - 1, 2 * WIN_W - 1
D_FF = D * 7 // 2
E = 8
TOP_K = 2
EPS = 1e-6
NQ = HEADS * HD
NKV = KV_HEADS * HD
QKV1 = NQ + 2 * NKV
MASKED = -1e30

COLS = 512
PK = 4
RAW = 6
SPLIT = 3
STEPS = D_FF // COLS
FFN_PIECES = 6 * STEPS

Q0 = 0
O0 = Q0 + 2 * (3 * D // COLS)
F0 = O0 + 2 * (D // COLS)
Q1 = F0 + FFN_PIECES
O1 = Q1 + 2 * (QKV1 // COLS)
J0 = O1 + 2 * (D // COLS)


C_IDENT, C_BEFORE, C_ONES, C_IOTA = 0, P, 2 * P, 3 * P
C_TRI = C_IOTA + SEQ
C_COS = C_TRI + E * E
C_SIN = C_COS + T * HD
C_ALL = C_SIN + T * HD


def constants():
    c = np.zeros((P, C_ALL), np.float32)
    c[:, C_IDENT:C_IDENT + P] = np.eye(P)
    c[:, C_IOTA:C_IOTA + SEQ] = np.arange(SEQ)
    c[:, C_BEFORE:C_BEFORE + P] = np.triu(np.ones((P, P)), 1)
    c[:, C_ONES:C_ONES + P] = 1.0
    c[:, C_TRI:C_TRI + E * E] = np.tril(np.ones((E, E)), -1).reshape(1, -1)
    quarter = HD // 4
    freqs = (np.float32(10000.0) ** (-np.arange(quarter, dtype=np.float32) / np.float32(quarter))).astype(np.float32)
    for t in range(T):
        tok = t * P + np.arange(P)
        for axis, pos in enumerate((tok // GRID_W, tok % GRID_W)):
            ang = pos.astype(np.float32)[:, None] * freqs[None, :]
            a = axis * HD // 2
            cos, sin = C_COS + t * HD + a, C_SIN + t * HD + a
            c[:, cos:cos + quarter] = c[:, cos + quarter:cos + 2 * quarter] = np.cos(ang)
            c[:, sin:sin + quarter] = -np.sin(ang)
            c[:, sin + quarter:sin + 2 * quarter] = np.sin(ang)
    return c


def first_piece(s):
    return 0 if s == 0 else 4 + 6 * (s - 1)


def encoder_kernel(nc, x, norm_g, na_w_qkv, na_rpb, na_w_o, gqa_w_qkv, gqa_q_norm, gqa_k_norm, gqa_w_o,
                   ffn_w_gate, ffn_w_up, ffn_w_down, moe_w_router, moe_w_gate, moe_w_up, moe_w_down,
                   consts, out):
    ctx = ExitStack()
    with ctx:
        def sb(name, shape, dt=F32, scope=None):
            return (scope or ctx).enter_context(nc.sbuf_tensor(name, shape, dt))

        def sem(name):
            return ctx.enter_context(nc.semaphore(name))

        raw = sb("raw", [P, RAW, PK, COLS])
        w_hi = sb("w_hi", [P, SPLIT, PK, COLS], F32R)
        w_lo = sb("w_lo", [P, SPLIT, PK, COLS], F32R)
        h = sb("h", [P, T, D])
        nrm = sb("nrm", [P, T, D])
        act_hi = sb("act_hi", [P, KC, SEQ], F32R)
        act_lo = sb("act_lo", [P, KC, SEQ], F32R)
        gain = sb("gain", [P, 2, D])
        cst = sb("cst", [P, C_ALL])
        wr = sb("wr", [P, KC, E])
        small = sb("small", [P, 64])
        junk = sb("junk", [P, D], mybir.dt.bfloat16)
        ident = cst[:, C_IDENT:C_IDENT + P]
        sumsq = small[:, 40:44].rearrange("p (t j) -> p t j", t=T)
        part, meansq, std, rstd = (small[:, 4 * i:4 * i + 2] for i in range(4))
        nmax = small[:, 16:24].rearrange("p (b s) -> p b s", b=2)
        psums = small[:, 24:32].rearrange("p (b s) -> p b s", b=2)
        pmax = small[:, 48:56].rearrange("p (b s) -> p b s", b=2)
        rsums = small[:, 32:40].rearrange("p (b s) -> p b s", b=2)
        attn = ExitStack()
        qT = sb("qT", [P, KC, SEQ], F32, attn)
        kT = sb("kT", [P, KC, SEQ], F32, attn)
        sc = sb("sc", [P, 2, 4, SEQ], F32, attn)
        pT = sb("pT", [P, 2, 8, P], F32, attn)
        layer0 = ExitStack()
        v0 = sb("v0", [P, T, D], F32, layer0)
        bias = sb("bias", [P, HEADS, ROWS + 2, GRID_W], F32, layer0)
        layer0.close()
        layer1 = ExitStack()
        qkv = sb("qkv", [P, T, QKV1], F32, layer1)
        rot_a = sb("rot_a", [P, T, COLS], F32, layer1)
        rot_b = sb("rot_b", [P, T, COLS], F32, layer1)
        kdup = sb("kdup", [P, T, KV_HEADS, 2, HD], F32, layer1)
        qk_gain = sb("qk_gain", [P, 2, HD], F32, layer1)
        qk_cos = sb("qk_cos", [P, 2, T, HD], F32, layer1)
        qk_sin = sb("qk_sin", [P, 2, T, HD], F32, layer1)
        head_ss = sb("head_ss", [P, 3, T, 8], F32, layer1)
        head_ms = sb("head_ms", [P, 3, T, 8], F32, layer1)
        head_std = sb("head_std", [P, 3, T, 8], F32, layer1)
        head_rs = sb("head_rs", [P, 3, T, 8], F32, layer1)
        layer1.close()
        attn.close()
        ffn = ExitStack()
        hid = sb("hid", [P, T, COLS], F32, ffn)
        sil = sb("sil", [P, T, COLS], F32, ffn)
        hT_hi = sb("hT_hi", [P, 2, T, PK * P], F32R, ffn)
        hT_lo = sb("hT_lo", [P, 2, T, PK * P], F32R, ffn)
        tok_hi = sb("tok_hi", [P, T, D], F32R, ffn)
        tok_lo = sb("tok_lo", [P, T, D], F32R, ffn)
        y_sb = sb("y_sb", [P, D], F32, ffn)
        routing = ExitStack()
        fT = sb("fT", [P, KC, SEQ], F32, routing)
        routing.close()
        second = ExitStack()
        y_sb2 = sb("y_sb2", [P, D], F32, second)
        pick_gT2 = sb("pick_gT2", [P, T, P], F32, second)
        second.close()
        last = ExitStack()
        scaled_sum = sb("scaled_sum", [P, T, D], F32, last)
        last.close()
        ffn.enter_context(nc.sbuf_tensor("under_fT", [P, KC, SEQ], F32))
        pick = sb("pick", [P, T, P], F32R, ffn)
        pick_g = sb("pick_g", [P, T, P], F32, ffn)
        pick_gT = sb("pick_gT", [P, T, P], F32, ffn)
        logit = sb("logit", [P, T, E], F32, ffn)
        pair = sb("pair", [P, T, E, E], F32, ffn)
        pair2 = sb("pair2", [P, T, E, E], F32, ffn)
        chosen = sb("chosen", [P, T, E], F32, ffn)
        gate = sb("gate", [P, T, E], F32, ffn)
        pos = sb("pos", [P, T, E], F32, ffn)
        neg_top = sb("neg_top", [P, T], F32, ffn)
        gate_sum = sb("gate_sum", [P, T], F32, ffn)
        gate_scale = sb("gate_scale", [P, T], F32, ffn)
        prod8 = sb("prod8", [P, T, E], F32, ffn)
        job_pos = sb("job_pos", [P, T, E], F32, ffn)
        job_gate = sb("job_gate", [P, T, E], F32, ffn)
        cur = sb("cur", [P, 2, T], F32, ffn)
        wide = sb("wide", [P, E], I32, ffn)
        ffn.close()
        ps = ctx.enter_context(nc.psum_tensor("ps", [P, 8, COLS], F32))

        landed = [sem(f"piece_landed_{i}") for i in range(RAW)]
        hi_ready, lo_ready, piece_used = sem("hi_ready"), sem("lo_ready"), sem("piece_used")
        x_in, cst_in, gain_in = [sem("x_in_0"), sem("x_in_1")], sem("cst_in"), [sem("gain_in_0"), sem("gain_in_1")]
        bias_in, bias_masked, qk_gain_in, wr_in = sem("bias_in"), sem("bias_masked"), sem("qk_gain_in"), sem("wr_in")
        ident_in, gain_used = sem("ident_in"), sem("gain_used")
        sumsq_ready, meansq_ready, std_ready = sem("sumsq_ready"), sem("meansq_ready"), sem("std_ready")
        nrm_ready, nrm_turned, act_hi_ready, act_ready = (
            sem("nrm_ready"), sem("nrm_turned"), sem("act_hi_ready"), sem("act_ready"))
        h_ready, tile0_done, scaled_ready = sem("h_ready"), sem("tile0_done"), sem("scaled_ready")
        dve_chain = sem("dve_chain")
        qkv_kept = [sem("qkv0_kept"), sem("qkv1_kept")]
        att = [{n: sem(f"{n}_{i}") for n in (
            "scores_ready", "biased", "max_ready", "exp_ready", "probs_ready", "probs_turned", "pT_ready",
            "o_ready", "o_hi_ready", "o_split")} for i in range(2)]
        heads_squared, heads_ms, heads_std, heads_ready, heads_turned, heads_kept = (
            sem("heads_squared"), sem("heads_ms"), sem("heads_std"), sem("heads_ready"), sem("heads_turned"),
            sem("heads_kept"))
        f0 = {n: sem(f"ffn_{n}") for n in ("silu", "hid", "turned", "hT_hi", "hT")}
        fj = {n: sem(f"job_{n}") for n in ("silu", "hid", "turned", "hT_hi", "hT")}
        tok_hi_ready, tok_ready, fT_ready, logits_ready = (
            sem("tok_hi_ready"), sem("tok_ready"), sem("fT_ready"), sem("logits_ready"))
        logits_kept, logits_exp, chosen_ready, pos_ready, wide_ready = (
            sem("logits_kept"), sem("logits_exp"), sem("chosen_ready"), sem("pos_ready"), sem("wide_ready"))
        cur_ready, pick_ready, gathered, x_hi_ready, x_ready = (
            sem("cur_ready"), sem("pick_ready"), sem("gathered"), sem("x_hi_ready"), sem("x_ready"))
        pick_turned, pickT_ready, y_kept, scattered, y_added = (
            sem("pick_turned"), sem("pickT_ready"), sem("y_kept"), sem("scattered"), sem("y_added"))
        pick2_ready, gathered2, x2_hi_ready, x2_ready, pick2_turned, pick2T_ready = (
            sem("pick2_ready"), sem("gathered2"), sem("x2_hi_ready"), sem("x2_ready"), sem("pick2_turned"),
            sem("pick2T_ready"))
        out_stored = sem("out_stored")

        def rows_of(ap):
            return ap.rearrange("p b (r c) -> p b r c", c=GRID_W)[:, :, :, ::-1]

        def outputs(layer, u, acts):
            a, t = u // 2, u % 2
            dst = acts[:, 2 * a:2 * a + 2, t * P:(t + 1) * P]
            src = ps[:, 6 + u % 2, 0:2 * P].rearrange("p (b n) -> p b n", b=2)
            if layer == 0:
                return dst.rearrange("p b (r c) -> p b r c", c=GRID_W), rows_of(src)
            return dst, src

        def is_first(j):
            return isinstance(j, int) and j == 0

        def is_last(j):
            return isinstance(j, int) and j == E - 1

        def by_width(eng, j, wide_job, narrow_job):
            is_wide = eng.value_load(wide[0:1, bass.ds(j, 1)], min_val=0, max_val=1)
            with eng.If(is_wide > 0):
                wide_job(j)
            with eng.Else():
                narrow_job(j)

        def all_jobs(eng, wide_job, narrow_job):
            by_width(eng, 0, wide_job, narrow_job)
            with eng.Fori(1, E - 1) as j:
                by_width(eng, j, wide_job, narrow_job)
            by_width(eng, E - 1, wide_job, narrow_job)

        def gates_of(s):
            return ps[:, 4:8:2, :] if s == 0 else ps[:, 0:4:2, :]

        def ups_of(s):
            return ps[:, 5:8:2, :] if s == 0 else ps[:, 1:4:2, :]

        def splits_before_turn(s):
            return first_piece(1) + 4 if s == 0 else min(first_piece(s) + 7, FFN_PIECES)

        def gathered_in(bank):
            banks = ps[:, 6:8, :] if bank == 6 else ps[:, 1:4:2, :]
            return banks.rearrange("p b (c n) -> p b c n", c=4)

        def slots(acts, t):
            return acts[:, :, t * P:(t + 1) * P].rearrange("p (b c) n -> p b c n", c=4)

        def w_piece(w, k0, c0):
            return w[k0:k0 + PK * P, c0:c0 + COLS].rearrange("(b p) n -> p b n", p=P)

        def columns_then_halves(w, columns):
            return [(w, half * PK * P, c0) for c0 in columns for half in range(2)]

        qkv1_columns = (NQ, 0, COLS)

        def swiglu_pieces(w_gate, w_up, w_down):
            pieces = []
            for s in range(STEPS + 1):
                if s < STEPS:
                    for w in (w_gate, w_up):
                        pieces += [(w, half * PK * P, s * COLS) for half in range(2)]
                if s >= 1:
                    pieces += [(w_down, (s - 1) * COLS, half * COLS) for half in range(2)]
            return pieces

        front = (columns_then_halves(na_w_qkv[0], range(0, 3 * D, COLS)) + columns_then_halves(na_w_o[0], (0, COLS))
                 + swiglu_pieces(ffn_w_gate[0], ffn_w_up[0], ffn_w_down[0])
                 + columns_then_halves(gqa_w_qkv[0], qkv1_columns) + columns_then_halves(gqa_w_o[0], (0, COLS)))
        assert len(front) == J0 and FFN_PIECES % RAW == 0 and FFN_PIECES % SPLIT == 0

        PRODUCTS = {1: (O0, 0, F0), 3: (Q1 - 2, 4, Q1), 5: (O1, 0, J0)}
        TURN_BANK = {0: 4, 2: 0, 4: 4, 6: 4}

        SUMS = {(0, 0, 0): 1, (0, 1, 0): 2, (7, 0, 0): 21, (7, 1, 0): 22}
        ROOTS = {(0, 0): 1, (0, 1): 2, (7, 0): 15, (7, 1): 16}
        for k in PRODUCTS:
            first = [(k, 0, 0), (k, 0, 1), (k + 1, 0, 0), (k, 1, 0)] if k == 3 else [
                (k, 0, 0), (k, 1, 0), (k, 0, 1), (k + 1, 0, 0)]
            for i, key in enumerate(first + [(k, 1, 1), (k + 1, 1, 0)]):
                SUMS[key] = 2 + 6 * (k // 2) + i + 1
            for i, key in enumerate([(k, 0), (k + 1, 0), (k, 1), (k + 1, 1)]):
                ROOTS[key] = 2 + 4 * (k // 2) + i + 1

        def half_count(k, t, half):
            return 2 * (T * (k // 2) + t) + half + 1

        def product_ready(k, t, j):
            n = PRODUCTS[k][0]
            if k == 3:
                return (tile0_done, 2 + j) if t == 0 else (piece_used, n + 1 + j)
            if j == 0:
                return piece_used, n + 2
            return (tile0_done, 1 if k == 1 else 4) if t == 0 else (piece_used, n + 4)

        block = ctx.enter_context(nc.Block())

        @block.sync
        def _(sp):
            def load(n, src, job=0):
                if not isinstance(n, int) or n >= RAW or not isinstance(job, int):
                    sp.wait_ge(lo_ready, job * FFN_PIECES + n - RAW + 1)
                sp.dma_start(raw[:, n % RAW, :, :], src).then_inc(landed[n % RAW], 16)

            def load_expert(job, expert):
                pieces = swiglu_pieces(moe_w_gate[0, expert], moe_w_up[0, expert], moe_w_down[0, expert])
                for i, piece in enumerate(pieces):
                    load(J0 + i, w_piece(*piece), job)

            for t in range(T):
                sp.dma_start(h[:, t, :], x[0, t * P:(t + 1) * P, :]).then_inc(x_in[t], 16)
            sp.dma_start(ident, consts[:, C_IDENT:C_IDENT + P]).then_inc(ident_in, 16)
            for n, piece in enumerate(front):
                load(n, w_piece(*piece))
            with sp.Fori(0, E) as e:
                load_expert(e, e)
            for t in range(T):
                sp.wait_ge(h_ready, 4 * T - T + t + 1)
                sp.dma_start(out[0, t * P:(t + 1) * P, :], h[:, t, :]).then_inc(out_stored, 16)
            sp.wait_ge(out_stored, 16 * T)

        @block.gpsimd
        def _(pool):
            def load_gain(k):
                if k >= 2:
                    pool.wait_ge(gain_used, k - 1)
                g = norm_g[k // 4, k % 4:k % 4 + 1, :]
                pool.dma_start(gain[:, k % 2, :], g.to_broadcast([P, D])).then_inc(gain_in[k % 2], 16)

            load_gain(0)
            load_gain(1)
            for a in range(2):
                for i in range(ROWS + 2):
                    src = bass.AP(na_rpb.tensor, (WIN_H - ROWS + 1 - a + i) * RPB_W + WIN_W - GRID_W,
                                  [[1, GRID_W], [RPB_H * RPB_W, HEADS], [1, GRID_W]])
                    pool.dma_start(bias[a * GRID_W:(a + 1) * GRID_W, :, i, :], src).then_inc(bias_in, 16)
            pool.wait_ge(bias_in, 2 * (ROWS + 2) * 16)
            edge = GRID_W - WIN_W
            for a in range(2):
                b = bias[a * GRID_W:(a + 1) * GRID_W].rearrange("p h i k -> p (h i) k")
                rows = HEADS * (ROWS + 2)
                pool.affine_select(out=b[:, :, 0:edge], in_=b[:, :, 0:edge], compare_op=ALU.is_ge, fill=MASKED,
                                   base=WIN_W // 2 - GRID_W + 1, pattern=[[0, rows], [1, edge]],
                                   channel_multiplier=1
                                   ).then_inc(bias_masked, 1)
                pool.wait_ge(bias_masked, 2 * a + 1)
                pool.affine_select(out=b[:, :, WIN_W:], in_=b[:, :, WIN_W:], compare_op=ALU.is_ge, fill=MASKED,
                                   base=WIN_W // 2 - 1 - WIN_W + GRID_W - 1, pattern=[[0, rows], [-1, edge]],
                                   channel_multiplier=-1).then_inc(bias_masked, 1)
            pool.dma_start(cst[:, P:], consts[:, P:]).then_inc(cst_in, 16)
            pool.dma_start(wr[:], moe_w_router[0].rearrange("(b p) e -> p b e", p=P)).then_inc(wr_in, 16)
            for k in range(2, 5):
                load_gain(k)
            for i, g in enumerate((gqa_q_norm, gqa_k_norm)):
                pool.dma_start(qk_gain[:, i, :], g.to_broadcast([P, HD])).then_inc(qk_gain_in, 16)
            for k in range(5, 8):
                load_gain(k)

        @block.scalar
        def _(act):
            split_at = [0]

            def split_until(end, job=None):
                for n in range(split_at[0], end):
                    base = 0 if job is None else job
                    act.wait_ge(landed[n % RAW], (base * (FFN_PIECES // RAW) + n // RAW + 1) * 16)
                    if n >= SPLIT:
                        act.wait_ge(piece_used, base * FFN_PIECES + n - SPLIT + 1)
                    act.activation(w_hi[:, n % SPLIT], raw[:, n % RAW], ACT.Copy).then_inc(hi_ready, 1)
                split_at[0] = max(end, split_at[0])

            def root(k, t):
                act.wait_ge(meansq_ready, ROOTS[k, t])
                act.activation(std[:, t:t + 1], meansq[:, t:t + 1], ACT.Sqrt).then_inc(std_ready, 1)

            def free_junk(k, t, j):
                if SUMS[k, t, j] > 1:
                    act.wait_ge(sumsq_ready, SUMS[k, t, j] - 1)

            def square_h(k, t):
                free_junk(k, t, 0)
                if k == 0:
                    act.wait_ge(x_in[t], 16)
                else:
                    act.wait_ge(h_ready, T * (k // 2) - T + t + 1)
                act.activation(junk[:], h[:, t, :], ACT.Square, accum_out=sumsq[:, t, 0:1]).then_inc(sumsq_ready, 1)

            def square_product(k, t, j):
                free_junk(k, t, j)
                sig, count = product_ready(k, t, j)
                act.wait_ge(sig, count)
                act.activation(junk[:, 0:COLS], ps[:, PRODUCTS[k][1] + 2 * t + j, :], ACT.Square,
                               accum_out=sumsq[:, t, j:j + 1]).then_inc(sumsq_ready, 1)

            def keep_turned(k, t):
                for half in range(2):
                    act.wait_ge(nrm_turned, half_count(k, t, half))
                    act.activation(act_hi[:, half * PK:(half + 1) * PK, t * P:(t + 1) * P],
                                   ps[:, TURN_BANK[k] + 2 * t + half, :].rearrange("p (c n) -> p c n", c=4), ACT.Copy
                                   ).then_inc(act_hi_ready, 1)

            def norms(k):
                after = PRODUCTS[k][2]
                act.preload_act_table(ACT.Sqrt)
                if k == 3:
                    split_until(after + 1)
                square_product(k, 0, 0)
                if k != 3:
                    square_product(k, 1, 0)
                    split_until(after + 1)
                square_product(k, 0, 1)
                root(k, 0)
                square_h(k + 1, 0)
                root(k + 1, 0)
                if k == 3:
                    square_product(k, 1, 0)
                square_product(k, 1, 1)
                if k == 5:
                    keep_fT(0)
                else:
                    keep_turned(k + 1, 0)
                root(k, 1)
                if k != 5:
                    split_until(after + 2)
                square_h(k + 1, 1)
                root(k + 1, 1)
                if k == 5:
                    keep_fT(1)
                else:
                    split_until(after + SPLIT)
                    keep_turned(k + 1, 1)

            def keep_fT(t):
                for half in range(2):
                    act.wait_ge(nrm_turned, half_count(6, t, half))
                    act.activation(fT[:, half * PK:(half + 1) * PK, t * P:(t + 1) * P],
                                   ps[:, 4 + 2 * t + half, :].rearrange("p (c n) -> p c n", c=4), ACT.Copy
                                   ).then_inc(fT_ready, 1)
                act.wait_ge(nrm_ready, T * 3 + t + 1)
                act.activation(tok_hi[:, t, :], nrm[:, t, :], ACT.Copy).then_inc(tok_hi_ready, 1)

            def keep_values(half):
                act.wait_ge(piece_used, Q0 + 10 + 2 * half)
                act.activation(v0[:, :, half * COLS:(half + 1) * COLS], ps[:, 4 + 2 * half:6 + 2 * half, :], ACT.Copy
                               ).then_inc(qkv_kept[0], 1)

            def attention(i, following, beside=lambda: None):
                s = att[i]
                units = 2 * HEADS // 4
                for u in range(units + 3):
                    if u >= 3:
                        act.wait_ge(s["o_ready"], u - 2)
                        dst, src = outputs(i, u - 3, act_hi)
                        act.activation(dst, src, ACT.Copy).then_inc(s["o_hi_ready"], 1)
                    if u < units:
                        act.wait_ge(s["max_ready"], u + 1)
                        if i == 1 and u >= 2:
                            act.wait_ge(s["probs_turned"], u - 1)
                        for q in range(4):
                            src = sc[:, u % 2, q, :] if i == 0 else ps[:, 2 * (u % 2) + q // 2,
                                                                      (q % 2) * SEQ:(q % 2 + 1) * SEQ]
                            last = act.activation(sc[:, u % 2, q, :], src, ACT.Exp, bias=nmax[:, u % 2, q:q + 1],
                                                  accum_out=psums[:, u % 2, q:q + 1])
                        last.then_inc(s["exp_ready"], 1)
                    if u == 1:
                        beside()
                    if 1 <= u <= units:
                        act.wait_ge(s["probs_turned"], u)
                        if u >= 3:
                            act.wait_ge(s["o_ready"], u - 2)
                        act.activation(pT[:, (u - 1) % 2].rearrange("p a n -> p (a n)"),
                                       ps[:, 4:6, :].rearrange("p b n -> p (b n)"), ACT.Copy
                                       ).then_inc(s["pT_ready"], 1)
                    if u < SPLIT:
                        split_until(following + u + 1)

            def swiglu_both_tiles(base, s_of, job=None):
                pieces, steps = (0, 0) if job is None else (job * FFN_PIECES, job * STEPS)
                for s in range(STEPS):
                    last = first_piece(s) + 3
                    split_until(base + last + 3, job)
                    act.wait_ge(piece_used, pieces + (base + last + 1))
                    act.activation(sil[:], gates_of(s), ACT.Silu).then_inc(s_of["silu"], 1)
                    split_until(base + splits_before_turn(s), job)
                    act.wait_ge(s_of["turned"], steps + s + 1)
                    act.activation(hT_hi[:, s % 2], gates_of(s), ACT.Copy).then_inc(s_of["hT_hi"], 1)
                split_until(base + FFN_PIECES, job)

            act.preload_act_table(ACT.Sqrt)
            for t in range(T):
                square_h(0, t)
                root(0, t)
            for t in range(T):
                keep_turned(0, t)
                split_until(t + 1)
            for j in range(4):
                split_until(Q0 + 2 * j + 4)
                act.wait_ge(piece_used, Q0 + 2 * j + 2)
                chunks = slice(4 * (j % 2), 4 * (j % 2) + 4)
                if j < 2:
                    act.activation(qT[:, chunks, :].rearrange("p b (r c) -> p b r c", c=GRID_W),
                                   rows_of(ps[:, chunks, 0:SEQ]), ACT.Copy, scale=HD ** -0.5
                                   ).then_inc(qkv_kept[0], 1)
                else:
                    act.activation(kT[:, chunks, :], ps[:, chunks, 0:SEQ], ACT.Copy).then_inc(qkv_kept[0], 1)
            split_until(O0)
            keep_values(0)
            act.preload_act_table(ACT.Exp)
            attention(0, O0, lambda: keep_values(1))
            split_until(F0)
            norms(1)
            act.preload_act_table(ACT.Silu)
            swiglu_both_tiles(F0, f0)
            norms(3)

            def keep_heads(j):
                act.wait_ge(heads_turned, j + 1)
                src = ps[:, 6:8, :].rearrange("p t (c n) -> p c t n", c=4)
                dst = kT[:, 0:KV_HEADS, :] if j == 0 else qT[:, 4 * (j - 1):4 * j, :]
                act.activation(dst.rearrange("p c (t n) -> p c t n", t=T), src, ACT.Copy).then_inc(heads_kept, 1)

            for j in range(3):
                heads = KV_HEADS if j == 0 else 8
                split_until(min(Q1 + 2 * j + 4, O1))
                act.wait_ge(piece_used, Q1 + 2 * j + 2)
                if j > 0:
                    act.wait_ge(heads_ready, j)
                act.activation(rot_b[:, :, 0:heads * HD], ps[:, 2 * j:2 * j + 2, 0:heads * HD], ACT.Square
                               ).then_inc(heads_squared, 1)
                c0 = qkv1_columns[j]
                act.activation(qkv[:, :, c0:c0 + COLS], ps[:, 2 * j:2 * j + 2, :], ACT.Copy).then_inc(qkv_kept[1], 1)
                if j > 0:
                    keep_heads(j - 1)
                act.wait_ge(heads_ms, j + 1)
                act.activation(head_std[:, j, :, 0:heads], head_ms[:, j, :, 0:heads], ACT.Sqrt).then_inc(heads_std, 1)
            act.preload_act_table(ACT.Exp)
            keep_heads(2)
            attention(1, O1)
            split_until(J0)
            norms(5)
            act.preload_act_table(ACT.Exp)
            act.wait_ge(logits_kept, 1)
            for t in range(T):
                act.activation(gate[:, t, :], logit[:, t, :], ACT.Exp, bias=neg_top[:, t:t + 1]).then_inc(logits_exp, 1)
            split_until(J0 + SPLIT)
            act.preload_act_table(ACT.Silu)

            def keep_gathered(j, bank=6):
                for half in range(2):
                    act.wait_ge(gathered, 2 * j + (half + 1))
                    act.activation(slots(act_hi, 0)[:, half], gathered_in(bank)[:, half], ACT.Copy
                                   ).then_inc(x_hi_ready, 1)

            def start_job(j):
                split_at[0] = J0 + SPLIT if is_first(j) else J0
                split_until(J0 + SPLIT, j)
                act.wait_ge(pick_turned, j + 1)
                if not is_first(j):
                    act.wait_ge(scattered, T * j)
                act.activation(pick_gT[:], ps[:, 1, 0:T * P].rearrange("p (t n) -> p t n", t=T), ACT.Copy
                               ).then_inc(pickT_ready, 1)

            def narrow_job(j):
                start_job(j)
                act.sem_inc(pick2T_ready, 1)
                act.sem_inc(x2_hi_ready, 1)
                for s in range(STEPS):
                    split_until(J0 + first_piece(s) + 6, j)
                    act.wait_ge(piece_used, j * FFN_PIECES + (J0 + first_piece(s) + 4))
                    act.activation(sil[:, 0, :], ps[:, 2 * (s % 2), :], ACT.Silu).then_inc(fj["silu"], 1)
                    split_until(J0 + min(first_piece(s + 1) + 4, FFN_PIECES - 1), j)
                    act.wait_ge(fj["turned"], j * STEPS + s + 1)
                    act.activation(hT_hi[:, 0, 0, :], ps[:, 2 * (s % 2), :], ACT.Copy).then_inc(fj["hT_hi"], 1)
                split_until(J0 + FFN_PIECES, j)
                if not is_last(j):
                    keep_gathered(j + 1)
                for half in range(2):
                    act.wait_ge(piece_used, j * FFN_PIECES + (J0 + FFN_PIECES - 1 + half))
                    act.activation(y_sb[:, half * COLS:(half + 1) * COLS], ps[:, 4 + half, :], ACT.Copy
                                   ).then_inc(y_kept, 1)

            def wide_job(j):
                start_job(j)
                act.wait_ge(pick2_turned, j + 1)
                act.activation(pick_gT2[:], ps[:, 1, 0:T * P].rearrange("p (t n) -> p t n", t=T), ACT.Copy
                               ).then_inc(pick2T_ready, 1)
                act.wait_ge(gathered2, 2 * j + 2)
                act.activation(slots(act_hi, 1), gathered_in(6), ACT.Copy).then_inc(x2_hi_ready, 1)
                swiglu_both_tiles(J0, fj, j)
                if not is_last(j):
                    keep_gathered(j + 1, 1)
                act.wait_ge(piece_used, j * FFN_PIECES + (J0 + FFN_PIECES))
                act.activation(y_sb[:], ps[:, 4:6, :].rearrange("p b n -> p (b n)"), ACT.Copy)
                act.activation(y_sb2[:], ps[:, 6:8, :].rearrange("p b n -> p (b n)"), ACT.Copy).then_inc(y_kept, 2)

            keep_gathered(0)
            act.wait_ge(wide_ready, 1)
            all_jobs(act, wide_job, narrow_job)
            act.preload_act_table(ACT.Sqrt)
            for t in range(T):
                free_junk(7, t, 0)
                act.wait_ge(y_added, E * T + t + 1)
                act.activation(junk[:], nrm[:, t, :], ACT.Square, accum_out=sumsq[:, t, 0:1]).then_inc(sumsq_ready, 1)
                root(7, t)

        @block.vector
        def _(dve):
            split_at = [0]
            links = [0]

            def link(ins):
                links[0] += 1
                ins.then_inc(dve_chain, 1)
                dve.wait_ge(dve_chain, links[0])

            def split_until(end, job=None):
                for n in range(split_at[0], end):
                    base = 0 if job is None else job
                    dve.wait_ge(hi_ready, base * FFN_PIECES + n + 1)
                    dve.tensor_tensor(w_lo[:, n % SPLIT], raw[:, n % RAW], w_hi[:, n % SPLIT].bitcast(F32),
                                      ALU.subtract).then_inc(lo_ready, 1)
                split_at[0] = max(end, split_at[0])

            def mean_square(k, t, first_half=None):
                dve.wait_ge(sumsq_ready, SUMS[k, t, 0 if first_half is None else 1])
                if first_half is None:
                    ins = dve.tensor_scalar(meansq[:, t:t + 1], sumsq[:, t, 0:1], 1.0 / D, EPS, ALU.mult, ALU.add)
                else:
                    ins = dve.tensor_scalar(meansq[:, t:t + 1], sumsq[:, t, 1:2], 1.0 / D, first_half,
                                            ALU.mult, ALU.add)
                ins.then_inc(meansq_ready, 1)

            def inverse(k, t):
                dve.wait_ge(std_ready, ROOTS[k, t])
                link(dve.reciprocal(rstd[:, t:t + 1], std[:, t:t + 1]))

            def normalise(k, t):
                inverse(k, t)
                dve.scalar_tensor_tensor(nrm[:, t, :], h[:, t, :], rstd[:, t:t + 1], gain[:, 0, :],
                                         ALU.mult, ALU.mult).then_inc(nrm_ready, 1)

            def keep_turned(k, t):
                for half in range(2):
                    dve.wait_ge(act_hi_ready, half_count(k, t, half))
                    blocks, tok = slice(half * PK, (half + 1) * PK), slice(t * P, (t + 1) * P)
                    dve.tensor_tensor(act_lo[:, blocks, tok],
                                      ps[:, TURN_BANK[k] + 2 * t + half, :].rearrange("p (c n) -> p c n", c=4),
                                      act_hi[:, blocks, tok].bitcast(F32), ALU.subtract).then_inc(act_ready, 1)

            def norms(k):
                n, bank, after = PRODUCTS[k]

                def scale(t, j):
                    dve.wait_ge(sumsq_ready, SUMS[k, t, j])
                    cols = slice(j * COLS, (j + 1) * COLS)
                    dve.tensor_tensor(nrm[:, t, cols], ps[:, bank + 2 * t + j, :], gain[:, 1, cols], ALU.mult
                                      ).then_inc(scaled_ready, 1)
                    if j == 0:
                        link(dve.tensor_scalar(part[:, t:t + 1], sumsq[:, t, 0:1], 1.0 / D, EPS, ALU.mult, ALU.add))

                def add(t, beside=lambda: None):
                    mean_square(k, t, part[:, t:t + 1])
                    scale(t, 1)
                    beside()
                    inverse(k, t)
                    done = 2 * T if t == 1 else 2 if k == 3 else 3
                    dve.wait_ge(scaled_ready, 2 * T * (k // 2) + done)
                    dve.scalar_tensor_tensor(h[:, t, :], nrm[:, t, :], rstd[:, t:t + 1], h[:, t, :],
                                             ALU.mult, ALU.add).then_inc(h_ready, 1)
                    dve.wait_ge(h_ready, T * (k // 2) + t + 1)

                dve.wait_ge(gain_in[1], 16 * (k // 2 + 1))
                dve.wait_ge(gain_in[0], 16 * ((k + 1) // 2 + 1))
                if k == 3:
                    split_until(after + 1)
                scale(0, 0)
                if k != 3:
                    scale(1, 0)
                    split_until(after + 1)
                add(0)
                mean_square(k + 1, 0)
                normalise(k + 1, 0)
                if k == 3:
                    scale(1, 0)
                add(1, lambda: k != 5 and keep_turned(k + 1, 0))
                if k != 5:
                    split_until(after + 2)
                mean_square(k + 1, 1)
                normalise(k + 1, 1)
                dve.wait_ge(nrm_ready, T * ((k + 1) // 2 + 1))
                dve.sem_inc(gain_used, 2)
                if k != 5:
                    split_until(after + SPLIT)
                    keep_turned(k + 1, 1)

            def attention(i, following):
                s = att[i]
                units = 2 * HEADS // 4
                for u in range(units + 3):
                    if u < units:
                        a, t = u // 2, u % 2
                        dve.wait_ge(s["scores_ready"], u + 1)
                        banks = ps[:, 2 * (u % 2):2 * (u % 2) + 2, :]
                        if i == 0:
                            if u >= 2:
                                dve.wait_ge(s["probs_turned"], u - 1)
                            for q in range(4):
                                par, b = q // 2, q % 2
                                link_max = dve.tensor_tensor_reduce(
                                    sc[:, u % 2, q, :], banks[:, par, b * SEQ:(b + 1) * SEQ],
                                    bias[:, 4 * a + par + 2 * b, 2 - 2 * t:6 - 2 * t, :].rearrange("p i n -> p (i n)"),
                                    1.0, -3e38, ALU.add, ALU.max, pmax[:, u % 2, q:q + 1])
                            link_max.then_inc(s["biased"], 1)
                            dve.wait_ge(s["biased"], u + 1)
                            dve.tensor_scalar(nmax[:, u % 2, :], pmax[:, u % 2, :], -1.0, None, ALU.mult
                                              ).then_inc(s["max_ready"], 1)
                        else:
                            dve.tensor_reduce(nmax[:, u % 2, :], banks.rearrange("p b (c n) -> p (b c) n", c=2),
                                              AX.X, ALU.max, negate=True).then_inc(s["max_ready"], 1)
                    if 1 <= u <= units:
                        half = (u - 1) % 2
                        dve.wait_ge(s["exp_ready"], u)
                        link(dve.reciprocal(rsums[:, half, :], psums[:, half, :]))
                        for q in range(4):
                            last = dve.tensor_scalar(sc[:, half, q, :], sc[:, half, q, :], rsums[:, half, q:q + 1],
                                                     None, ALU.mult)
                        last.then_inc(s["probs_ready"], 1)
                    if u >= 3:
                        dve.wait_ge(s["o_hi_ready"], u - 2)
                        lo, src = outputs(i, u - 3, act_lo)
                        hi, _ = outputs(i, u - 3, act_hi.bitcast(F32))
                        dve.tensor_tensor(lo, src, hi, ALU.subtract).then_inc(s["o_split"], 1)
                    if 1 <= u <= SPLIT:
                        split_until(following + u)

            def head_tables():
                dve.wait_ge(cst_in, 16)
                dve.wait_ge(qk_gain_in, 32)
                for g, scale in enumerate((HD ** -0.5, 1.0)):
                    for t in range(T):
                        cos = cst[:, C_COS + t * HD:C_COS + (t + 1) * HD]
                        sin = cst[:, C_SIN + t * HD:C_SIN + (t + 1) * HD].rearrange("p (a b f) -> p a b f", a=2, b=2)
                        swapped = qk_sin[:, g, t, :].rearrange("p (a b f) -> p a b f", a=2, b=2)
                        other = qk_gain[:, g, :].rearrange("p (a b f) -> p a b f", a=2, b=2)
                        link(dve.scalar_tensor_tensor(qk_cos[:, g, t, :], cos, scale, qk_gain[:, g, :],
                                                      ALU.mult, ALU.mult))
                        for b in range(2):
                            link(dve.scalar_tensor_tensor(swapped[:, :, b, :], sin[:, :, b, :], scale,
                                                          other[:, :, 1 - b, :], ALU.mult, ALU.mult))

            def rotate_heads(j):
                n = KV_HEADS if j == 0 else 8
                g = 1 if j == 0 else 0
                c0 = qkv1_columns[j]
                own = qkv[:, :, c0:c0 + n * HD].rearrange("p t (n d) -> p t n d", d=HD)
                ra = rot_a[:, :, 0:n * HD].rearrange("p t (n d) -> p t n d", d=HD)
                rb = rot_b[:, :, 0:n * HD].rearrange("p t (n d) -> p t n d", d=HD)
                dve.wait_ge(heads_squared, j + 1)
                link(dve.tensor_reduce(head_ss[:, j, :, 0:n], rb, AX.X, ALU.add))
                dve.tensor_scalar(head_ms[:, j, :, 0:n], head_ss[:, j, :, 0:n], 1.0 / HD, EPS, ALU.mult, ALU.add
                                  ).then_inc(heads_ms, 1)
                dve.wait_ge(qkv_kept[1], j + 1)
                dve.tensor_tensor(ra, own, qk_cos[:, g].unsqueeze(2).to_broadcast([P, T, n, HD]), ALU.mult)
                for t in range(T):
                    x = own[:, t].rearrange("p n (a b f) -> p n a b f", a=2, b=2)
                    o = rb[:, t].rearrange("p n (a b f) -> p n a b f", a=2, b=2)
                    sin = qk_sin[:, g, t, :].rearrange("p (a b f) -> p a b f", a=2, b=2)
                    for b in range(2):
                        last = dve.tensor_tensor(o[:, :, :, b, :], x[:, :, :, 1 - b, :],
                                                 sin[:, :, b, :].unsqueeze(1).to_broadcast([P, n, 2, HD // 4]),
                                                 ALU.mult)
                link(last)
                link(dve.tensor_tensor(ra, ra, rb, ALU.add))
                dve.wait_ge(heads_std, j + 1)
                link(dve.reciprocal(head_rs[:, j, :, 0:n], head_std[:, j, :, 0:n]))
                rs = head_rs[:, j, :, 0:n].unsqueeze(3).to_broadcast([P, T, n, HD])
                if j == 0:
                    for copy in range(2):
                        last = dve.tensor_tensor(kdup[:, :, :, copy, :], ra, rs, ALU.mult)
                else:
                    last = dve.tensor_tensor(own, ra, rs, ALU.mult)
                last.then_inc(heads_ready, 1)

            def swiglu_both_tiles(base, s_of, job=None):
                steps = 0 if job is None else job * STEPS
                for s in range(STEPS):
                    last = first_piece(s) + 3
                    split_until(base + last + 3, job)
                    dve.wait_ge(s_of["silu"], steps + s + 1)
                    dve.tensor_tensor(hid[:], sil[:], ups_of(s), ALU.mult).then_inc(s_of["hid"], 1)
                    split_until(base + splits_before_turn(s), job)
                    if s == STEPS - 1 and job is not None and not is_last(job):
                        build_pick(job + 1, pick2_turned)
                    dve.wait_ge(s_of["hT_hi"], steps + s + 1)
                    dve.tensor_tensor(hT_lo[:, s % 2], gates_of(s), hT_hi[:, s % 2].bitcast(F32), ALU.subtract
                                      ).then_inc(s_of["hT"], 1)
                split_until(base + FFN_PIECES, job)

            for t in range(T):
                mean_square(0, t)
                if t == 0:
                    dve.wait_ge(gain_in[0], 16)
                normalise(0, t)
            dve.wait_ge(nrm_ready, T)
            dve.sem_inc(gain_used, 1)
            for t in range(T):
                keep_turned(0, t)
                split_until(t + 1)
            split_until(O0)
            dve.wait_ge(bias_masked, 4)
            attention(0, O0)
            split_until(F0)
            norms(1)
            swiglu_both_tiles(F0, f0)
            norms(3)
            head_tables()
            for j in range(3):
                split_until(min(Q1 + 2 * j + 4, O1))
                rotate_heads(j)
            attention(1, O1)
            split_until(J0)
            norms(5)

            for t in range(T):
                dve.wait_ge(tok_hi_ready, t + 1)
                dve.tensor_tensor(tok_lo[:, t, :], nrm[:, t, :], tok_hi[:, t, :].bitcast(F32), ALU.subtract
                                  ).then_inc(tok_ready, 1)
            dve.wait_ge(logits_ready, 1)
            link(dve.tensor_copy(logit[:], ps[:, 0, 0:T * E].rearrange("p (t e) -> p t e", t=T)))
            dve.tensor_reduce(neg_top[:], logit[:], AX.X, ALU.max, negate=True).then_inc(logits_kept, 1)
            tri = cst[:, C_TRI:C_TRI + E * E]
            lj = logit[:].unsqueeze(2).to_broadcast([P, T, E, E])
            le = logit[:].unsqueeze(3).to_broadcast([P, T, E, E])
            dve.tensor_tensor(pair[:], lj, le, ALU.is_gt)
            link(dve.tensor_tensor(pair2[:], lj, le, ALU.is_equal))
            ties = pair2[:].rearrange("p t e j -> p t (e j)")
            link(dve.tensor_tensor(ties, ties, tri.unsqueeze(1).to_broadcast([P, T, E * E]), ALU.mult))
            link(dve.tensor_tensor(pair[:], pair[:], pair2[:], ALU.add))
            link(dve.tensor_reduce(prod8[:], pair[:], AX.X, ALU.add))
            dve.tensor_scalar(chosen[:], prod8[:], float(TOP_K), None, ALU.is_lt).then_inc(chosen_ready, 1)
            dve.wait_ge(chosen_ready, 1)
            dve.wait_ge(logits_exp, T)
            link(dve.tensor_tensor(gate[:], gate[:], chosen[:], ALU.mult))
            link(dve.tensor_reduce(gate_sum[:], gate[:], AX.X, ALU.add))
            link(dve.reciprocal(gate_scale[:], gate_sum[:]))
            for t in range(T):
                link(dve.tensor_scalar(job_gate[:, t, :], gate[:, t, :], gate_scale[:, t:t + 1], None, ALU.mult))
            dve.wait_ge(pos_ready, 1)
            link(dve.scalar_tensor_tensor(pos[:], ps[:, 1, 0:T * E].rearrange("p (t e) -> p t e", t=T), 1.0,
                                          chosen[:], ALU.add, ALU.mult))
            dve.tensor_scalar(wide[:], ps[:, 1, T * E:(T + 1) * E], float(P), None, ALU.is_gt).then_inc(wide_ready, 1)
            link(dve.tensor_scalar(job_pos[:], pos[:], -1.0, None, ALU.add))

            def one_hot(first_slot, ready):
                iota = cst[:, C_IOTA + first_slot:C_IOTA + first_slot + P]
                for t in range(T):
                    dve.tensor_scalar(pick[:, t, :], iota, cur[:, 0, t:t + 1], None, ALU.is_equal
                                      ).then_inc(ready, 1)
                for t in range(T):
                    dve.tensor_scalar(pick_g[:, t, :], iota, cur[:, 0, t:t + 1], cur[:, 1, t:t + 1],
                                      ALU.is_equal, ALU.mult).then_inc(ready, 1)

            def build_pick(j, used=None):
                if used is not None:
                    dve.wait_ge(used, j)
                column = bass.ds(j, 1)
                dve.tensor_copy(cur[:, 0, :].unsqueeze(2), job_pos[:, :, column]).then_inc(cur_ready, 1)
                dve.tensor_copy(cur[:, 1, :].unsqueeze(2), job_gate[:, :, column]).then_inc(cur_ready, 1)
                dve.wait_ge(cur_ready, 2 * j + 2)
                one_hot(0, pick_ready)

            def keep_gathered(j, bank=6):
                for half in range(2):
                    dve.wait_ge(x_hi_ready, 2 * j + (half + 1))
                    dve.tensor_tensor(slots(act_lo, 0)[:, half], gathered_in(bank)[:, half],
                                      slots(act_hi.bitcast(F32), 0)[:, half], ALU.subtract).then_inc(x_ready, 1)

            def add_outputs(j):
                for t, b in enumerate((4, 2)):
                    dve.wait_ge(scattered, T * j + (t + 1))
                    dve.tensor_tensor(nrm[:, t, :], nrm[:, t, :],
                                      ps[:, b:b + 2, :].rearrange("p b n -> p (b n)"), ALU.add).then_inc(y_added, 1)

            def start_job(j, pieces_first):
                split_at[0] = J0 + SPLIT if is_first(j) else J0
                split_until(J0 + pieces_first, j)
                if not is_first(j):
                    dve.wait_ge(y_added, T * j)
                    add_outputs(j - 1)

            def narrow_job(j):
                start_job(j, SPLIT)
                dve.sem_inc(pick2_ready, 4)
                dve.sem_inc(x2_ready, 1)
                for s in range(STEPS):
                    split_until(J0 + first_piece(s) + 6, j)
                    dve.wait_ge(fj["silu"], j * STEPS + s + 1)
                    dve.tensor_tensor(hid[:, 0, :], sil[:, 0, :], ps[:, 2 * (s % 2) + 1, :], ALU.mult
                                      ).then_inc(fj["hid"], 1)
                    if s == STEPS - 1 and not is_last(j):
                        build_pick(j + 1, pick_turned)
                    split_until(J0 + min(first_piece(s + 1) + 4, FFN_PIECES - 1), j)
                    dve.wait_ge(fj["hT_hi"], j * STEPS + s + 1)
                    dve.tensor_tensor(hT_lo[:, 0, 0, :], ps[:, 2 * (s % 2), :], hT_hi[:, 0, 0, :].bitcast(F32),
                                      ALU.subtract).then_inc(fj["hT"], 1)
                split_until(J0 + FFN_PIECES, j)
                if not is_last(j):
                    keep_gathered(j + 1)

            def wide_job(j):
                start_job(j, 1)
                dve.wait_ge(pick_turned, j + 1)
                one_hot(P, pick2_ready)
                split_until(J0 + SPLIT, j)
                dve.wait_ge(x2_hi_ready, j + 1)
                dve.tensor_tensor(slots(act_lo, 1), gathered_in(6), slots(act_hi.bitcast(F32), 1), ALU.subtract
                                  ).then_inc(x2_ready, 1)
                swiglu_both_tiles(J0, fj, j)
                if not is_last(j):
                    keep_gathered(j + 1, 1)

            build_pick(0)
            dve.wait_ge(nrm_turned, half_count(6, T - 1, 1))
            dve.wait_ge(tok_ready, T)
            for t in range(T):
                dve.memset(nrm[:, t, :], 0.0).then_inc(y_added, 1)
            split_until(J0 + SPLIT)
            keep_gathered(0)
            all_jobs(dve, wide_job, narrow_job)
            dve.wait_ge(y_added, E * T)
            add_outputs(E - 1)
            dve.wait_ge(gain_in[1], 16 * 4)
            for t in range(T):
                dve.wait_ge(y_added, (E + 1) * T - T + t + 1)
                dve.tensor_tensor(scaled_sum[:, t, :], nrm[:, t, :], gain[:, 1, :], ALU.mult).then_inc(scaled_ready, 1)
                mean_square(7, t)
            for t in range(T):
                inverse(7, t)
                dve.wait_ge(scaled_ready, 2 * T * 3 + t + 1)
                dve.scalar_tensor_tensor(h[:, t, :], scaled_sum[:, t, :], rstd[:, t:t + 1], h[:, t, :],
                                         ALU.mult, ALU.add).then_inc(h_ready, 1)

        @block.tensor
        def _(pe):
            def product(out, hi, lo, slot, b, start, stop):
                wh, wl = w_hi[:, slot, b, :], w_lo[:, slot, b, :]
                pe.matmul(out, hi, wh, start=start, stop=False)
                pe.matmul(out, hi, wl, start=False, stop=False)
                return pe.matmul(out, lo, wh, start=False, stop=stop)

            def take(n, job=None):
                pe.wait_ge(lo_ready, (0 if job is None else job * FFN_PIECES) + n + 1)

            def turn_norm(k, t):
                if k == 0 and t == 0:
                    pe.wait_ge(ident_in, 16)
                pe.wait_ge(nrm_ready, T * (k // 2) + t + 1)
                for c in range(KC):
                    ins = pe.transpose(ps[:, TURN_BANK[k] + 2 * t + c // 4, (c % 4) * P:(c % 4 + 1) * P],
                                       nrm[:, t, c * P:(c + 1) * P], ident)
                    if c % 4 == 3:
                        ins.then_inc(nrm_turned, 1)

            def token_blocks(n, half, t, bank):
                for b in range(PK):
                    c = PK * half + b
                    tok = slice(t * P, (t + 1) * P)
                    last = product(ps[:, bank, :], act_hi[:, c, tok], act_lo[:, c, tok], n % SPLIT, b,
                                   c == 0, c == KC - 1)
                return last

            def two_pieces(n, banks, job=None):
                for half in range(2):
                    take(n + half, job)
                    for t in range(T):
                        last = token_blocks(n + half, half, t, banks(t))
                    last.then_inc(piece_used, 1)

            def four_pieces_turning(n, first, second, k):
                turn_norm(k, 0)
                for half in range(2):
                    pe.wait_ge(act_ready, half_count(k, 0, half))
                    take(n + half)
                    token_blocks(n + half, half, 0, first(0))
                turn_norm(k, 1)
                take(n + 2)
                token_blocks(n + 2, 0, 0, second(0))
                for half in range(2):
                    pe.wait_ge(act_ready, half_count(k, 1, half))
                    token_blocks(n + half, half, 1, first(1)).then_inc(piece_used, 1)
                token_blocks(n + 2, 0, 1, second(1)).then_inc(piece_used, 1)
                take(n + 3)
                for t in range(T):
                    last = token_blocks(n + 3, 1, t, second(t))
                last.then_inc(piece_used, 1)

            def output_product(n):
                two_pieces(n, lambda t: 2 * t)
                for t in range(T):
                    for half in range(2):
                        if t == 0:
                            take(n + 2 + half)
                        last = token_blocks(n + 2 + half, half, t, 2 * t + 1)
                        if t == 1:
                            last.then_inc(piece_used, 1)
                    if t == 0:
                        last.then_inc(tile0_done, 1)

            def attention(i, kv_chunk, value, beside, values_ready):
                s = att[i]
                units = 2 * HEADS // 4

                def scores(u):
                    a, t = u // 2, u % 2
                    if u >= 2:
                        pe.wait_ge(s["biased"] if i == 0 else s["exp_ready"], u - 1)
                    for b in range(2):
                        for par in range(2):
                            head = 4 * a + 2 * b + par
                            rows = slice(par * HD, (par + 1) * HD)
                            last = pe.matmul(ps[:, 2 * (u % 2) + par, b * SEQ:(b + 1) * SEQ],
                                             qT[rows, head // 2, t * P:(t + 1) * P],
                                             kT[rows, kv_chunk(head), :], start=True, stop=True)
                    last.then_inc(s["scores_ready"], 1)

                scores(0)
                for u in range(units + 2):
                    if u == 1:
                        beside()
                    if u + 1 < units:
                        scores(u + 1)
                    if 1 <= u <= units:
                        pe.wait_ge(s["probs_ready"], u)
                        if u >= 2:
                            pe.wait_ge(s["pT_ready"], u - 1)
                        for q in range(4):
                            for c in range(2):
                                m = 2 * (q % 2) + c
                                last = pe.transpose(ps[:, 4 + q // 2, m * P:(m + 1) * P],
                                                    sc[:, (u - 1) % 2, q, c * P:(c + 1) * P], ident)
                        last.then_inc(s["probs_turned"], 1)
                    if u >= 2:
                        w = u - 2
                        if w == 0:
                            values_ready()
                        pe.wait_ge(s["pT_ready"], w + 1)
                        if w >= 2:
                            pe.wait_ge(s["o_split"], w - 1)
                        for q in range(4):
                            par, b = q // 2, q % 2
                            head = 4 * (w // 2) + 2 * b + par
                            for c in range(2):
                                last = pe.matmul(ps[par * HD:(par + 1) * HD, 6 + w % 2, b * P:(b + 1) * P],
                                                 value(c, head), pT[:, w % 2, 2 * q + c, :],
                                                 start=(c == 0), stop=(c == 1))
                        last.then_inc(s["o_ready"], 1)

            def down_blocks(n, s, half, buf, t, bank):
                for b in range(PK):
                    last = product(ps[:, bank + half, :], hT_hi[:, buf, t, b * P:(b + 1) * P],
                                   hT_lo[:, buf, t, b * P:(b + 1) * P], n % SPLIT, b,
                                   s == 0 and b == 0, s == STEPS - 1 and b == PK - 1)
                return last

            def swiglu_both_tiles(base, s_of, first_step, job=None):
                steps = 0 if job is None else job * STEPS

                def turn(s):
                    pe.wait_ge(s_of["hid"], steps + s + 1)
                    for t in range(T):
                        for b in range(PK):
                            last = pe.transpose(ps[:, (4 if s == 0 else 0) + 2 * t, b * P:(b + 1) * P],
                                                hid[:, t, b * P:(b + 1) * P], ident)
                    last.then_inc(s_of["turned"], 1)

                first_step(base)
                for s in range(1, STEPS):
                    n = base + first_piece(s)
                    if s > 1:
                        pe.wait_ge(s_of["hT"], steps + s)
                    two_pieces(n, lambda t: 2 * t, job)
                    if s == 1:
                        turn(0)
                    two_pieces(n + 2, lambda t: 2 * t + 1, job)
                    if s == 1:
                        pe.wait_ge(s_of["hT"], steps + 1)
                    for half in range(2):
                        if half == 1:
                            turn(s)
                        take(n + 4 + half, job)
                        for t in range(T):
                            last = down_blocks(n + 4 + half, s - 1, half, (s - 1) % 2, t, 4 + 2 * t)
                        last.then_inc(piece_used, 1)

            for t in range(T):
                turn_norm(0, t)
            for j in range(4):
                if j >= 2:
                    pe.wait_ge(qkv_kept[0], j - 1)
                for half in range(2):
                    if j == 0:
                        pe.wait_ge(act_ready, half_count(0, T - 1, half))
                    n = Q0 + 2 * j + half
                    take(n)
                    for b in range(PK):
                        c = PK * half + b
                        for m in range(4):
                            o = ps[:, 4 * (j % 2) + m, 0:SEQ]
                            wh = w_hi[:, n % SPLIT, b, m * P:(m + 1) * P]
                            wl = w_lo[:, n % SPLIT, b, m * P:(m + 1) * P]
                            pe.matmul(o, wh, act_hi[:, c, :], start=(c == 0), stop=False)
                            pe.matmul(o, wh, act_lo[:, c, :], start=False, stop=False)
                            last = pe.matmul(o, wl, act_hi[:, c, :], start=False, stop=(c == KC - 1))
                    last.then_inc(piece_used, 1)
            pe.wait_ge(qkv_kept[0], 4)
            two_pieces(Q0 + 8, lambda t: 4 + t)
            attention(0, lambda head: head // 2, lambda c, head: v0[:, c, head * HD:(head + 1) * HD],
                      lambda: two_pieces(Q0 + 10, lambda t: 6 + t), lambda: pe.wait_ge(qkv_kept[0], 6))
            pe.wait_ge(att[0]["o_split"], 8)
            output_product(O0)

            swiglu_both_tiles(F0, f0, lambda n: four_pieces_turning(n, lambda t: 4 + 2 * t, lambda t: 5 + 2 * t, 2))
            pe.wait_ge(f0["hT"], STEPS)
            for t in range(T):
                for half in range(2):
                    n = Q1 - 2 + half
                    if t == 0:
                        take(n)
                    last = down_blocks(n, STEPS - 1, half, (STEPS - 1) % 2, t, 4 + 2 * t)
                    last.then_inc(tile0_done if t == 0 else piece_used, 1)

            def turn_heads(j):
                pe.wait_ge(heads_ready, j + 1)
                if j > 0:
                    pe.wait_ge(heads_kept, j)
                for t in range(T):
                    for c in range(4):
                        if j == 0:
                            src = kdup[:, t, c].rearrange("p a d -> p (a d)")
                        else:
                            src = qkv[:, t, qkv1_columns[j] + c * P:qkv1_columns[j] + (c + 1) * P]
                        last = pe.transpose(ps[:, 6 + t, c * P:(c + 1) * P], src, ident)
                last.then_inc(heads_turned, 1)

            four_pieces_turning(Q1, lambda t: t, lambda t: 2 + t, 4)
            turn_heads(0)
            two_pieces(Q1 + 4, lambda t: 4 + t)
            turn_heads(1)
            pe.wait_ge(heads_kept, 2)

            def last_heads():
                turn_heads(2)
                pe.wait_ge(heads_kept, 3)

            v_at = NQ + NKV
            attention(1, lambda head: head // 4,
                      lambda c, head: qkv[:, c, v_at + (head // 4) * HD:v_at + (head // 4 + 1) * HD],
                      last_heads, lambda: None)
            pe.wait_ge(att[1]["o_split"], 8)
            output_product(O1)

            pe.wait_ge(wr_in, 16)
            for t in range(T):
                turn_norm(6, t)
                for c in range(KC):
                    if c % PK == 0:
                        pe.wait_ge(fT_ready, 2 * t + c // PK + 1)
                    last = pe.matmul(ps[:, 0, t * E:(t + 1) * E], fT[:, c, t * P:(t + 1) * P], wr[:, c, :],
                                     start=(c == 0), stop=(c == KC - 1))
            last.then_inc(logits_ready, 1)
            pe.wait_ge(chosen_ready, 1)
            before, ones = cst[:, C_BEFORE:C_BEFORE + P], cst[:, C_ONES:C_ONES + P]
            pe.matmul(ps[:, 1, 0:E], before, chosen[:, 0, :], start=True, stop=True)
            pe.matmul(ps[:, 1, E:2 * E], ones, chosen[:, 0, :], start=True, stop=False)
            pe.matmul(ps[:, 1, E:2 * E], before, chosen[:, 1, :], start=False, stop=True)
            pe.matmul(ps[:, 1, 2 * E:3 * E], ones, chosen[:, 0, :], start=True, stop=False)
            pe.matmul(ps[:, 1, 2 * E:3 * E], ones, chosen[:, 1, :], start=False, stop=True).then_inc(pos_ready, 1)

            def gather_slots(banks, signal):
                for c in range(KC):
                    o = ps[:, banks[c // 4], (c % 4) * P:(c % 4 + 1) * P]
                    for t in range(T):
                        pe.matmul(o, tok_hi[:, t, c * P:(c + 1) * P], pick[:, t, :], start=(t == 0), stop=False)
                        last = pe.matmul(o, tok_lo[:, t, c * P:(c + 1) * P], pick[:, t, :], start=False,
                                         stop=(t == T - 1))
                    if c % 4 == 3:
                        last.then_inc(signal, 1)

            def gather(j, banks=(6, 7)):
                pe.wait_ge(pick_ready, 4 * j + T)
                gather_slots(banks, gathered)

            def turn_pick(signal, ready, j):
                pe.wait_ge(ready, 4 * j + 4)
                for t in range(T):
                    last = pe.transpose(ps[:, 1, t * P:(t + 1) * P], pick_g[:, t, :], ident)
                last.then_inc(signal, 1)

            def scatter(parts):
                for t, bank in enumerate((4, 2)):
                    for half in range(2):
                        for i, (to_token, y) in enumerate(parts):
                            last = pe.matmul(ps[:, bank + half, :], to_token[:, t, :],
                                             y[:, half * COLS:(half + 1) * COLS],
                                             start=(i == 0), stop=(i == len(parts) - 1))
                    last.then_inc(scattered, 1)

            def narrow_job(j):
                pe.sem_inc(gathered2, 2)
                pe.sem_inc(pick2_turned, 1)
                for s in range(STEPS):
                    n = J0 + first_piece(s)
                    q = 2 * (s % 2)
                    if s == 1:
                        pe.wait_ge(y_added, T * j + T)
                    for m in range(4):
                        if s == 0 and m == 2:
                            pe.wait_ge(pickT_ready, j + 1)
                        if s == 0 and m < 2:
                            pe.wait_ge(x_ready, 2 * j + (m + 1))
                        take(n + m, j)
                        token_blocks(n + m, m % 2, 0, q + m // 2).then_inc(piece_used, 1)
                        if m == 1 and s >= 1:
                            turn_hidden(j, s - 1)
                    if s >= 1:
                        pe.wait_ge(fj["hT"], j * STEPS + s)
                        for half in range(2):
                            take(n + 4 + half, j)
                            down_blocks(n + 4 + half, s - 1, half, 0, 0, 4).then_inc(piece_used, 1)
                turn_hidden(j, STEPS - 1)
                if not is_last(j):
                    gather(j + 1)
                pe.wait_ge(fj["hT"], j * STEPS + STEPS)
                for half in range(2):
                    n = J0 + FFN_PIECES - 2 + half
                    take(n, j)
                    down_blocks(n, STEPS - 1, half, 0, 0, 4).then_inc(piece_used, 1)
                pe.wait_ge(y_kept, 2 * j + 2)
                scatter([(pick_gT, y_sb)])
                if not is_last(j):
                    turn_pick(pick_turned, pick_ready, j + 1)

            def wide_job(j):
                def first_step(n):
                    for half in range(2):
                        pe.wait_ge(x_ready, 2 * j + (half + 1))
                        take(n + half, j)
                        token_blocks(n + half, half, 0, 4)
                    pe.wait_ge(pick2_ready, 4 * j + T)
                    gather_slots((6, 7), gathered2)
                    pe.wait_ge(pickT_ready, j + 1)
                    turn_pick(pick2_turned, pick2_ready, j)
                    take(n + 2, j)
                    token_blocks(n + 2, 0, 0, 5)
                    pe.wait_ge(x2_ready, j + 1)
                    for half in range(2):
                        token_blocks(n + half, half, 1, 6).then_inc(piece_used, 1)
                    token_blocks(n + 2, 0, 1, 7).then_inc(piece_used, 1)
                    take(n + 3, j)
                    for t in range(T):
                        last = token_blocks(n + 3, 1, t, 5 + 2 * t)
                    last.then_inc(piece_used, 1)
                    pe.wait_ge(pick2T_ready, j + 1)

                pe.wait_ge(y_added, T * j + T)
                swiglu_both_tiles(J0, fj, first_step, j)
                pe.wait_ge(fj["hT"], j * STEPS + STEPS)
                if not is_last(j):
                    gather(j + 1, (1, 3))
                for half in range(2):
                    n = J0 + FFN_PIECES - 2 + half
                    take(n, j)
                    for t in range(T):
                        last = down_blocks(n, STEPS - 1, half, (STEPS - 1) % 2, t, 4 + 2 * t)
                    last.then_inc(piece_used, 1)
                if not is_last(j):
                    pe.wait_ge(x_ready, 2 * j + 4)
                pe.wait_ge(y_kept, 2 * j + 2)
                scatter([(pick_gT, y_sb), (pick_gT2, y_sb2)])
                if not is_last(j):
                    turn_pick(pick_turned, pick_ready, j + 1)

            def turn_hidden(j, s):
                pe.wait_ge(fj["hid"], j * STEPS + s + 1)
                for b in range(PK):
                    last = pe.transpose(ps[:, 2 * (s % 2), b * P:(b + 1) * P], hid[:, 0, b * P:(b + 1) * P], ident)
                last.then_inc(fj["turned"], 1)

            pe.wait_ge(tok_ready, T)
            gather(0)
            turn_pick(pick_turned, pick_ready, 0)
            pe.wait_ge(wide_ready, 1)
            all_jobs(pe, wide_job, narrow_job)


_INS = ["x", "norm_g", "na_w_qkv", "na_rpb", "na_w_o", "gqa_w_qkv", "gqa_q_norm", "gqa_k_norm", "gqa_w_o",
        "ffn_w_gate", "ffn_w_up", "ffn_w_down", "moe_w_router", "moe_w_gate", "moe_w_up", "moe_w_down"]


def kernel(**inputs):
    import concourse.bacc as bacc
    from concourse.bass_utils import run_bass_kernel_spmd

    nc = bacc.Bacc("TRN2", target_bir_lowering=False, num_devices=1)
    arrays, args = {}, []
    for name in _INS:
        a = np.ascontiguousarray(inputs[name])
        arrays[f"in_{name}"] = a
        args.append(nc.dram_tensor(f"in_{name}", a.shape, mybir.dt.from_np(a.dtype), kind="ExternalInput").ap())
    arrays["in_consts"] = constants()
    args.append(nc.dram_tensor("in_consts", (P, C_ALL), F32, kind="ExternalInput").ap())
    args.append(nc.dram_tensor("out_0", (1, SEQ, D), F32, kind="ExternalOutput").ap())
    encoder_kernel(nc, *args)
    r = run_bass_kernel_spmd(nc, [arrays], core_ids=[0])
    return r.results[0]["out_0"]
```
